# Optimizing a Trainium2 kernel written in Bass

```python
import math
import jax
import jax.numpy as jnp
from jax import lax
import numpy as np
import jax, jax.numpy as jnp

D_MODEL = 2048
BATCH = 1
SEQ = 256
DEPTH = 1

MIX_WIDTH = D_MODEL
ATTN_HEAD_DIM = 128
ATTN_WIDTH = MIX_WIDTH // 2
ATTN_HEADS = ATTN_WIDTH // ATTN_HEAD_DIM
MOBA_BLOCK = 256
MOBA_TOPK = 3
MOBA_QCHUNK = 32
REL_BUCKETS = 32
REL_MAX_DIST = 128
SSM_WIDTH = MIX_WIDTH - ATTN_WIDTH
SSM_HEAD_DIM = 64
SSM_HEADS = SSM_WIDTH // SSM_HEAD_DIM
SSM_GROUPS = 2
SSM_HEADS_PER_GROUP = SSM_HEADS // SSM_GROUPS
SSM_STATE = 128
SSM_CONV = 4
SSM_CHUNK = 128
SSM_CONV_CH = SSM_WIDTH + 2 * SSM_GROUPS * SSM_STATE
IN_COLS = 3 * ATTN_WIDTH + SSM_WIDTH + SSM_CONV_CH + SSM_HEADS
FFN_HIDDEN = 256 * (-(-8 * D_MODEL // (3 * 256)))
FFN_CONV = 3
NORM_EPS = 1e-6
NEG = -1e30


def rms_norm(x, w):
    xf = x.astype(jnp.float32)
    y = xf * lax.rsqrt(jnp.mean(xf * xf, axis=-1, keepdims=True) + NORM_EPS)
    return (y * w.astype(jnp.float32)).astype(x.dtype)

def causal_depthwise_conv(x, w, b):
    k = w.shape[0]
    y = lax.conv_general_dilated(x, w[:, None, :].astype(x.dtype), window_strides=(1,), padding=[(k - 1, 0)],
                                 dimension_numbers=('NWC', 'WIO', 'NWC'), feature_group_count=x.shape[-1])
    return y + b.astype(x.dtype)

def t5_bucket(rel):
    n = jnp.maximum(rel, 0)
    max_exact = REL_BUCKETS // 2
    nf = jnp.maximum(n, 1).astype(jnp.float32)
    large = max_exact + (jnp.log(nf / max_exact) / math.log(REL_MAX_DIST / max_exact)
                         * (REL_BUCKETS - max_exact)).astype(jnp.int32)
    large = jnp.minimum(large, REL_BUCKETS - 1)
    return jnp.where(n < max_exact, n, large)

def moba_attention(q, k, v, rel_bias):
    bsz, s, h, dh = q.shape
    nb = -(-s // MOBA_BLOCK)
    pad = nb * MOBA_BLOCK - s
    n_sel = min(MOBA_TOPK, nb - 1)
    scale = dh ** -0.5
    qh = q.transpose(0, 2, 1, 3)
    kh = jnp.pad(k.transpose(0, 2, 1, 3), ((0, 0), (0, 0), (0, pad), (0, 0)))
    vh = jnp.pad(v.transpose(0, 2, 1, 3), ((0, 0), (0, 0), (0, pad), (0, 0)))
    kb = kh.reshape(bsz, h, nb, MOBA_BLOCK, dh)
    vb = vh.reshape(bsz, h, nb, MOBA_BLOCK, dh)
    bias_h = rel_bias.T
    nqc = s // MOBA_QCHUNK
    q_chunks = qh.reshape(bsz, h, nqc, MOBA_QCHUNK, dh).transpose(2, 0, 1, 3, 4)
    t_blk = jnp.arange(MOBA_BLOCK)
    b_idx = jnp.arange(bsz)[:, None, None, None]
    h_idx = jnp.arange(h)[None, :, None, None]
    kmean = kb.mean(axis=3) if n_sel > 0 else None

    def one_chunk(args):
        c, qc = args
        q0 = c * MOBA_QCHUNK
        qpos = q0 + jnp.arange(MOBA_QCHUNK)
        own = q0 // MOBA_BLOCK
        k_own = lax.dynamic_slice_in_dim(kh, own * MOBA_BLOCK, MOBA_BLOCK, axis=2)
        v_own = lax.dynamic_slice_in_dim(vh, own * MOBA_BLOCK, MOBA_BLOCK, axis=2)
        rel_own = qpos[:, None] - (own * MOBA_BLOCK + t_blk)[None, :]
        lg_own = (jnp.einsum('bhqd,bhtd->bhqt', qc, k_own) * scale).astype(jnp.float32) \
            + bias_h[:, t5_bucket(rel_own)].astype(jnp.float32)
        lg_own = jnp.where(rel_own >= 0, lg_own, NEG)
        if n_sel == 0:
            p_own = jax.nn.softmax(lg_own, axis=-1).astype(v.dtype)
            return jnp.einsum('bhqt,bhtd->bhqd', p_own, v_own)
        gate = jnp.einsum('bhqd,bhnd->bhqn', qc, kmean).astype(jnp.float32)
        gate = jnp.where(jnp.arange(nb) < own, gate, NEG)
        _, idx = lax.top_k(gate, n_sel)
        valid = idx < own
        k_sel = kb[b_idx, h_idx, idx]
        v_sel = vb[b_idx, h_idx, idx]
        rel_sel = qpos[None, None, :, None, None] - (idx[..., None] * MOBA_BLOCK + t_blk)
        lg_sel = (jnp.einsum('bhqd,bhqjtd->bhqjt', qc, k_sel) * scale).astype(jnp.float32) \
            + bias_h[h_idx[..., None], t5_bucket(rel_sel)].astype(jnp.float32)
        lg_sel = jnp.where(valid[..., None], lg_sel, NEG)
        n_g = n_sel * MOBA_BLOCK
        lg = jnp.concatenate([lg_sel.reshape(bsz, h, MOBA_QCHUNK, n_g), lg_own], axis=-1)
        p = jax.nn.softmax(lg, axis=-1).astype(v.dtype)
        p_sel = p[..., :n_g].reshape(bsz, h, MOBA_QCHUNK, n_sel, MOBA_BLOCK)
        return jnp.einsum('bhqjt,bhqjtd->bhqd', p_sel, v_sel) + jnp.einsum('bhqt,bhtd->bhqd', p[..., n_g:], v_own)

    out = lax.map(one_chunk, (jnp.arange(nqc), q_chunks))
    return out.transpose(1, 0, 3, 2, 4).reshape(bsz, s, h * dh)

def ssd_chunked(x, dt, a, bm, cm):
    bsz, s, g, hg, p = x.shape
    n = bm.shape[-1]
    L = SSM_CHUNK
    nc = s // L
    xc = (x * dt[..., None]).reshape(bsz, nc, L, g, hg, p)
    a_cs = jnp.cumsum((dt * a).reshape(bsz, nc, L, g, hg), axis=2)
    bc = bm.reshape(bsz, nc, L, g, n)
    cc = cm.reshape(bsz, nc, L, g, n)
    seg = a_cs[:, :, :, None] - a_cs[:, :, None, :]
    causal = jnp.tril(jnp.ones((L, L), dtype=bool))[:, :, None, None]
    decay = jnp.exp(jnp.where(causal, seg, -jnp.inf))
    cb = jnp.einsum('bclgn,bcsgn->bclsg', cc, bc)
    y_diag = jnp.einsum('bclsg,bclsgh,bcsghp->bclghp', cb, decay, xc)
    decay_states = jnp.exp(a_cs[:, :, -1:] - a_cs)
    states = jnp.einsum('bclgn,bclgh,bclghp->bcghpn', bc, decay_states, xc)
    chunk_decay = jnp.exp(a_cs[:, :, -1])

    def step(hstate, inp):
        st, dec = inp
        return hstate * dec[..., None, None] + st, hstate

    _, prev = lax.scan(step, jnp.zeros_like(states[:, 0]),
                       (jnp.moveaxis(states, 1, 0), jnp.moveaxis(chunk_decay, 1, 0)))
    prev = jnp.moveaxis(prev, 0, 1)
    y_off = jnp.einsum('bclgn,bcghpn,bclgh->bclghp', cc, prev, jnp.exp(a_cs))
    return (y_diag + y_off).reshape(bsz, s, g, hg, p)

def mamba2_mixer(z, xbc, dt_raw, conv_w, conv_b, dt_bias, a_log, d_skip, norm_w):
    bsz, s, _ = z.shape
    f32 = jnp.float32
    xbc = jax.nn.silu(causal_depthwise_conv(xbc, conv_w, conv_b))
    xs, bm, cm = jnp.split(xbc, [SSM_WIDTH, SSM_WIDTH + SSM_GROUPS * SSM_STATE], axis=-1)
    xs = xs.reshape(bsz, s, SSM_GROUPS, SSM_HEADS_PER_GROUP, SSM_HEAD_DIM).astype(f32)
    bm = bm.reshape(bsz, s, SSM_GROUPS, SSM_STATE).astype(f32)
    cm = cm.reshape(bsz, s, SSM_GROUPS, SSM_STATE).astype(f32)
    dt = jax.nn.softplus(dt_raw.astype(f32) + dt_bias.astype(f32)).reshape(bsz, s, SSM_GROUPS, SSM_HEADS_PER_GROUP)
    a = -jnp.exp(a_log.astype(f32)).reshape(SSM_GROUPS, SSM_HEADS_PER_GROUP)
    y = ssd_chunked(xs, dt, a, bm, cm) + d_skip.astype(f32).reshape(SSM_GROUPS, SSM_HEADS_PER_GROUP, 1) * xs
    gw = SSM_WIDTH // SSM_GROUPS
    y = y.reshape(bsz, s, SSM_GROUPS, gw) * jax.nn.silu(z.astype(f32)).reshape(bsz, s, SSM_GROUPS, gw)
    y = y * lax.rsqrt(jnp.mean(y * y, axis=-1, keepdims=True) + NORM_EPS)
    return (y.reshape(bsz, s, SSM_WIDTH) * norm_w.astype(f32)).astype(z.dtype)

def first_inputs(seed: int = 0) -> dict:
    key = jax.random.key(seed)
    ks = jax.random.split(key, 18)
    f32 = jnp.float32

    def normal(k, shape, scale):
        return jax.random.normal(k, shape, f32) * scale

    def gain(k, width):
        return 1.0 + normal(k, (DEPTH, width), 0.02)

    x = normal(ks[0], (BATCH, SEQ, D_MODEL), 1.0)
    rel_bias = normal(ks[1], (REL_BUCKETS, ATTN_HEADS), 0.5)
    ln_mix_pre = gain(ks[2], D_MODEL)
    w_in = normal(ks[3], (DEPTH, D_MODEL, IN_COLS), D_MODEL ** -0.5)
    ssm_conv_w = normal(ks[4], (DEPTH, SSM_CONV, SSM_CONV_CH), SSM_CONV ** -0.5)
    ssm_conv_b = normal(ks[5], (DEPTH, SSM_CONV_CH), 0.02)
    dt0 = jnp.exp(jax.random.uniform(ks[6], (DEPTH, SSM_HEADS), f32, math.log(1e-3), math.log(1e-1)))
    dt_bias = dt0 + jnp.log(-jnp.expm1(-dt0))
    a_log = jnp.log(jax.random.uniform(ks[7], (DEPTH, SSM_HEADS), f32, 1.0, 16.0))
    d_skip = 1.0 + normal(ks[8], (DEPTH, SSM_HEADS), 0.1)
    ssm_norm_w = gain(ks[9], SSM_WIDTH)
    w_out = normal(ks[10], (DEPTH, MIX_WIDTH, D_MODEL), MIX_WIDTH ** -0.5)
    ln_mix_post = gain(ks[11], D_MODEL)
    ln_ffn_pre = gain(ks[12], D_MODEL)
    w_ffn_up = normal(ks[13], (DEPTH, D_MODEL, 2 * FFN_HIDDEN), D_MODEL ** -0.5)
    ffn_conv_w = normal(ks[14], (DEPTH, FFN_CONV, 2 * FFN_HIDDEN), FFN_CONV ** -0.5)
    ffn_conv_b = normal(ks[15], (DEPTH, 2 * FFN_HIDDEN), 0.02)
    w_ffn_down = normal(ks[16], (DEPTH, FFN_HIDDEN, D_MODEL), FFN_HIDDEN ** -0.5)
    ln_ffn_post = gain(ks[17], D_MODEL)
    return {'x': x, 'rel_bias': rel_bias, 'ln_mix_pre': ln_mix_pre, 'w_in': w_in,
            'ssm_conv_w': ssm_conv_w, 'ssm_conv_b': ssm_conv_b, 'dt_bias': dt_bias, 'a_log': a_log,
            'd_skip': d_skip, 'ssm_norm_w': ssm_norm_w, 'w_out': w_out, 'ln_mix_post': ln_mix_post,
            'ln_ffn_pre': ln_ffn_pre, 'w_ffn_up': w_ffn_up, 'ffn_conv_w': ffn_conv_w,
            'ffn_conv_b': ffn_conv_b, 'w_ffn_down': w_ffn_down, 'ln_ffn_post': ln_ffn_post}

def first_block(x, rel_bias, ln_mix_pre, w_in, ssm_conv_w, ssm_conv_b, dt_bias, a_log, d_skip,
              ssm_norm_w, w_out, ln_mix_post, ln_ffn_pre, w_ffn_up, ffn_conv_w, ffn_conv_b,
              w_ffn_down, ln_ffn_post):
    bsz, s, _ = x.shape
    aw, sw = ATTN_WIDTH, SSM_WIDTH
    splits = [aw, 2 * aw, 3 * aw, 3 * aw + sw, 3 * aw + sw + SSM_CONV_CH]
    for l in range(DEPTH):
        h = rms_norm(x, ln_mix_pre[l])
        proj = h @ w_in[l]
        q, k, v, z, xbc, dt_raw = jnp.split(proj, splits, axis=-1)
        shp = (bsz, s, ATTN_HEADS, ATTN_HEAD_DIM)
        attn = moba_attention(q.reshape(shp), k.reshape(shp), v.reshape(shp), rel_bias)
        ssm = mamba2_mixer(z, xbc, dt_raw, ssm_conv_w[l], ssm_conv_b[l], dt_bias[l], a_log[l],
                           d_skip[l], ssm_norm_w[l])
        mixed = jnp.concatenate([attn, ssm], axis=-1) @ w_out[l]
        x = x + rms_norm(mixed, ln_mix_post[l])
        h = rms_norm(x, ln_ffn_pre[l])
        u = causal_depthwise_conv(h @ w_ffn_up[l], ffn_conv_w[l], ffn_conv_b[l])
        gate, up = jnp.split(u, [FFN_HIDDEN], axis=-1)
        f = (jax.nn.gelu(gate, approximate=True) * up) @ w_ffn_down[l]
        x = x + rms_norm(f, ln_ffn_post[l])
    return x


GRID_W = 64
MIX_W = D_MODEL
RWKV_W = MIX_W // 2
ATTN_W = MIX_W - RWKV_W
HEAD_DIM = 64
RWKV_HEADS = RWKV_W // HEAD_DIM
ATTN_Q_HEADS = ATTN_W // HEAD_DIM
ATTN_KV_HEADS = 4
KV_GROUPS = ATTN_Q_HEADS // ATTN_KV_HEADS
KV_W = ATTN_KV_HEADS * HEAD_DIM
DECAY_LORA = 96
AAA_LORA = 96
GATE_LORA = 256
GN_EPS = 64e-5
ROPE_THETA = 10000.0
ROPE_AXIS_DIM = HEAD_DIM // 2
Q_BLOCK = 128
PEER_HEADS = 8
PEER_KEY_DIM = 256
PEER_HALF = PEER_KEY_DIM // 2
N_KEYS = 128
N_EXPERTS = N_KEYS * N_KEYS
PEER_TOPK = 16
PEER_CHUNK = 128

RWKV_SPLITS = (RWKV_W, 2 * RWKV_W, 3 * RWKV_W,
               3 * RWKV_W + DECAY_LORA, 3 * RWKV_W + 2 * DECAY_LORA,
               3 * RWKV_W + 2 * DECAY_LORA + AAA_LORA, 3 * RWKV_W + 2 * DECAY_LORA + 2 * AAA_LORA)
RWKV_COLS = 3 * RWKV_W + 2 * DECAY_LORA + 2 * AAA_LORA + GATE_LORA
IN_SPLITS = (RWKV_COLS, RWKV_COLS + ATTN_W, RWKV_COLS + ATTN_W + KV_W)
IN_COLS_2 = RWKV_COLS + ATTN_W + 2 * KV_W


def rmsnorm(x, w):
    xf = x.astype(jnp.float32)
    y = xf * lax.rsqrt(jnp.mean(xf * xf, axis=-1, keepdims=True) + NORM_EPS)
    return (y * w.astype(jnp.float32)).astype(x.dtype)

def centred_shift(z, mu_prev, mu_next):
    zp = jnp.pad(z[:, :-1], ((0, 0), (1, 0), (0, 0)))
    zn = jnp.pad(z[:, 1:], ((0, 0), (0, 1), (0, 0)))
    return z + mu_prev * (zp - z) + mu_next * (zn - z)

def rwkv7_bidir(z, mu_prev, mu_next, w0, w2, a0, a2, g2, k_k, k_a, r_k, lnx_w, lnx_b):
    B, S, _ = z.shape
    H, N = RWKV_HEADS, HEAD_DIM
    f32 = jnp.float32
    z = centred_shift(z.astype(f32), mu_prev.astype(f32), mu_next.astype(f32))
    r, k, v, wl_f, wl_b, al_f, al_b, gl = jnp.split(z, RWKV_SPLITS, axis=-1)
    wl = jnp.stack([wl_f, wl_b])
    al = jnp.stack([al_f, al_b])
    w_log = -jax.nn.softplus(-(w0.astype(f32)[:, None, None, :]
                               + jnp.einsum('nbsl,nlc->nbsc', jnp.tanh(wl), w2.astype(f32)))) - 0.5
    decay = jnp.exp(-jnp.exp(w_log))
    a = jax.nn.sigmoid(a0.astype(f32)[:, None, None, :]
                       + jnp.einsum('nbsl,nlc->nbsc', al, a2.astype(f32)))
    g = jax.nn.sigmoid(gl) @ g2.astype(f32)
    kk = (k * k_k.astype(f32)).reshape(B, S, H, N)
    kk = kk / jnp.maximum(jnp.sqrt(jnp.sum(kk * kk, axis=-1, keepdims=True)), 1e-12)
    kk = kk.reshape(B, S, RWKV_W)
    k_dir = k[None] * (1.0 + (a - 1.0) * k_a.astype(f32))
    ka = kk[None] * a

    def dir_seq(arr):
        arr = jnp.stack([arr[0], arr[1][:, ::-1]])
        return jnp.moveaxis(arr.reshape(2, B, S, H, N), 2, 0)

    xs = (dir_seq(jnp.stack([r, r])), dir_seq(decay), dir_seq(k_dir),
          dir_seq(jnp.stack([v, v])), dir_seq(jnp.stack([kk, kk])), dir_seq(ka))

    def step(state, inp):
        r_t, w_t, k_t, v_t, kk_t, ka_t = inp
        sa = jnp.einsum('dbhij,dbhj->dbhi', state, -kk_t)
        state = (state * w_t[..., None, :] + sa[..., :, None] * ka_t[..., None, :]
                 + v_t[..., :, None] * k_t[..., None, :])
        y = jnp.einsum('dbhij,dbhj->dbhi', state, r_t)
        return state, y

    state0 = jnp.zeros((2, B, H, N, N), f32)
    _, ys = lax.scan(step, state0, xs)
    ys = jnp.moveaxis(ys, 0, 2)
    y = ys[0] + ys[1][:, ::-1]
    mu = jnp.mean(y, axis=-1, keepdims=True)
    var = jnp.mean(jnp.square(y - mu), axis=-1, keepdims=True)
    y = ((y - mu) * lax.rsqrt(var + GN_EPS)).reshape(B, S, RWKV_W)
    y = y * lnx_w.astype(f32) + lnx_b.astype(f32)
    k_mean = jnp.mean(k_dir, axis=0).reshape(B, S, H, N)
    bonus = jnp.sum(r.reshape(B, S, H, N) * k_mean * r_k.astype(f32), axis=-1, keepdims=True) \
        * v.reshape(B, S, H, N)
    return (y + bonus.reshape(B, S, RWKV_W)) * g

def axial_rope_tables(S):
    rows_count = S // GRID_W
    rows = jnp.repeat(jnp.arange(rows_count), GRID_W).astype(jnp.float32)
    cols = jnp.tile(jnp.arange(GRID_W), rows_count).astype(jnp.float32)
    inv = ROPE_THETA ** (-jnp.arange(0, ROPE_AXIS_DIM, 2, dtype=jnp.float32) / ROPE_AXIS_DIM)
    ang_r = rows[:, None] * inv[None]
    ang_c = cols[:, None] * inv[None]
    return jnp.cos(ang_r), jnp.sin(ang_r), jnp.cos(ang_c), jnp.sin(ang_c)

def rope_rotate(x, cos, sin):
    x1, x2 = jnp.split(x, 2, axis=-1)
    c, s = cos[None, :, None, :], sin[None, :, None, :]
    return jnp.concatenate([x1 * c - x2 * s, x2 * c + x1 * s], axis=-1)

def axial_rope(x, tabs):
    cr, sr, cc, sc = tabs
    xr, xc = x[..., :ROPE_AXIS_DIM], x[..., ROPE_AXIS_DIM:]
    return jnp.concatenate([rope_rotate(xr, cr, sr), rope_rotate(xc, cc, sc)], axis=-1)

def axial_gqa(q, k, v, q_norm_w, k_norm_w):
    B, S, _ = q.shape
    dt = q.dtype
    q = q.reshape(B, S, ATTN_Q_HEADS, HEAD_DIM)
    k = k.reshape(B, S, ATTN_KV_HEADS, HEAD_DIM)
    v = v.reshape(B, S, ATTN_KV_HEADS, HEAD_DIM)
    tabs = axial_rope_tables(S)
    q = axial_rope(rmsnorm(q, q_norm_w).astype(jnp.float32), tabs) * (HEAD_DIM ** -0.5)
    k = axial_rope(rmsnorm(k, k_norm_w).astype(jnp.float32), tabs)
    q = q.astype(dt).reshape(B, S // Q_BLOCK, Q_BLOCK, ATTN_KV_HEADS, KV_GROUPS, HEAD_DIM)
    q = jnp.moveaxis(q, 1, 0)
    k = k.astype(dt)

    def block(q_blk):
        s = jnp.einsum('bqkgd,bskd->bkgqs', q_blk, k).astype(jnp.float32)
        p = jax.nn.softmax(s, axis=-1)
        return jnp.einsum('bkgqs,bskd->bqkgd', p.astype(v.dtype), v)

    o = lax.map(block, q)
    return jnp.moveaxis(o, 0, 1).reshape(B, S, ATTN_W)

def peer_ffn(h, w_pq, sub_keys, u_tab, v_tab):
    B, S, Dm = h.shape
    T = B * S
    hf = h.reshape(T, Dm)
    q = (hf @ w_pq).reshape(T, PEER_HEADS, 2, PEER_HALF)
    s = jnp.einsum('thpc,hpnc->thpn', q, sub_keys).astype(jnp.float32)
    s1, i1 = lax.top_k(s[:, :, 0], PEER_TOPK)
    s2, i2 = lax.top_k(s[:, :, 1], PEER_TOPK)
    cand = (s1[..., :, None] + s2[..., None, :]).reshape(T, PEER_HEADS, PEER_TOPK * PEER_TOPK)
    best, ci = lax.top_k(cand, PEER_TOPK)
    e1 = jnp.take_along_axis(i1, ci // PEER_TOPK, axis=-1)
    e2 = jnp.take_along_axis(i2, ci % PEER_TOPK, axis=-1)
    expert = (e1 * N_KEYS + e2).reshape(T, PEER_HEADS * PEER_TOPK)
    gate = jax.nn.softmax(best, axis=-1).reshape(T, PEER_HEADS * PEER_TOPK).astype(h.dtype)
    nc = T // PEER_CHUNK

    def chunk(args):
        hc, ec, gc = args
        u = jnp.take(u_tab, ec, axis=0)
        act = jax.nn.gelu(jnp.einsum('cd,ckd->ck', hc, u), approximate=False) * gc
        vv = jnp.take(v_tab, ec, axis=0)
        return jnp.einsum('ck,ckd->cd', act, vv)

    out = lax.map(chunk, (hf.reshape(nc, PEER_CHUNK, Dm),
                          expert.reshape(nc, PEER_CHUNK, -1),
                          gate.reshape(nc, PEER_CHUNK, -1)))
    return out.reshape(B, S, Dm)

def second_inputs(seed: int = 0) -> dict:
    key = jax.random.key(seed)
    ks = jax.random.split(key, 32)
    L, D, C = DEPTH, D_MODEL, RWKV_W
    nrm = lambda k, shape, scale: jax.random.normal(k, shape, jnp.float32) * scale
    return {
        "x": nrm(ks[0], (BATCH, SEQ, D), 1.0),
        "w_in": nrm(ks[1], (L, D, IN_COLS_2), D ** -0.5),
        "mu_prev": jax.random.uniform(ks[2], (L, RWKV_COLS), jnp.float32, 0.0, 0.5),
        "mu_next": jax.random.uniform(ks[3], (L, RWKV_COLS), jnp.float32, 0.0, 0.5),
        "w0": jax.random.uniform(ks[4], (L, 2, C), jnp.float32, -6.0, -1.0),
        "w2": nrm(ks[5], (L, 2, DECAY_LORA, C), 0.5 * DECAY_LORA ** -0.5),
        "a0": nrm(ks[6], (L, 2, C), 0.1),
        "a2": nrm(ks[7], (L, 2, AAA_LORA, C), AAA_LORA ** -0.5),
        "g2": nrm(ks[8], (L, GATE_LORA, C), GATE_LORA ** -0.5),
        "k_k": 0.85 + nrm(ks[9], (L, C), 0.05),
        "k_a": 1.0 + nrm(ks[10], (L, C), 0.05),
        "r_k": nrm(ks[11], (L, RWKV_HEADS, HEAD_DIM), 0.1),
        "lnx_w": 1.0 + nrm(ks[12], (L, C), 0.02),
        "lnx_b": nrm(ks[13], (L, C), 0.01),
        "q_norm_w": 1.0 + nrm(ks[14], (L, HEAD_DIM), 0.02),
        "k_norm_w": 1.0 + nrm(ks[15], (L, HEAD_DIM), 0.02),
        "w_out": nrm(ks[16], (L, MIX_W, D), MIX_W ** -0.5),
        "norm1_w": 1.0 + nrm(ks[17], (L, D), 0.02),
        "norm2_w": 1.0 + nrm(ks[18], (L, D), 0.02),
        "w_pq": nrm(ks[19], (L, D, PEER_HEADS * PEER_KEY_DIM), D ** -0.5),
        "sub_keys": nrm(ks[20], (L, PEER_HEADS, 2, N_KEYS, PEER_HALF), PEER_HALF ** -0.5),
        "u_tab": nrm(ks[21], (L, N_EXPERTS, D), D ** -0.5),
        "v_tab": nrm(ks[22], (L, N_EXPERTS, D), 0.1),
        "normf_w": 1.0 + nrm(ks[23], (D,), 0.02),
    }

def second_block(x, w_in, mu_prev, mu_next, w0, w2, a0, a2, g2, k_k, k_a, r_k, lnx_w, lnx_b,
              q_norm_w, k_norm_w, w_out, norm1_w, norm2_w, w_pq, sub_keys, u_tab, v_tab, normf_w):
    for l in range(DEPTH):
        h = rmsnorm(x, norm1_w[l])
        p = h @ w_in[l]
        z_rwkv, q, k, v = jnp.split(p, IN_SPLITS, axis=-1)
        y_rwkv = rwkv7_bidir(z_rwkv, mu_prev[l], mu_next[l], w0[l], w2[l], a0[l], a2[l], g2[l],
                             k_k[l], k_a[l], r_k[l], lnx_w[l], lnx_b[l]).astype(x.dtype)
        y_attn = axial_gqa(q, k, v, q_norm_w[l], k_norm_w[l])
        x = x + jnp.concatenate([y_rwkv, y_attn], axis=-1) @ w_out[l]
        h2 = rmsnorm(x, norm2_w[l])
        x = x + peer_ffn(h2, w_pq[l], sub_keys[l], u_tab[l], v_tab[l])
    return rmsnorm(x, normf_w)


def setup_inputs(seed=0):
    out = dict(first_inputs(seed))
    for name, value in second_inputs(seed + 1).items():
        if name != "x":
            out[name + "_2"] = value
    return out


def reference(
    x, rel_bias, ln_mix_pre, w_in, ssm_conv_w, ssm_conv_b, dt_bias, a_log, d_skip, ssm_norm_w,
    w_out, ln_mix_post, ln_ffn_pre, w_ffn_up, ffn_conv_w, ffn_conv_b, w_ffn_down, ln_ffn_post,
    w_in_2, mu_prev_2, mu_next_2, w0_2, w2_2, a0_2, a2_2, g2_2, k_k_2, k_a_2, r_k_2, lnx_w_2,
    lnx_b_2, q_norm_w_2, k_norm_w_2, w_out_2, norm1_w_2, norm2_w_2, w_pq_2, sub_keys_2, u_tab_2,
    v_tab_2, normf_w_2,
):
    x = first_block(
        x, rel_bias, ln_mix_pre, w_in, ssm_conv_w, ssm_conv_b, dt_bias, a_log, d_skip,
        ssm_norm_w, w_out, ln_mix_post, ln_ffn_pre, w_ffn_up, ffn_conv_w, ffn_conv_b,
        w_ffn_down, ln_ffn_post,
    )
    return second_block(
        x, w_in_2, mu_prev_2, mu_next_2, w0_2, w2_2, a0_2, a2_2, g2_2, k_k_2, k_a_2, r_k_2,
        lnx_w_2, lnx_b_2, q_norm_w_2, k_norm_w_2, w_out_2, norm1_w_2, norm2_w_2, w_pq_2,
        sub_keys_2, u_tab_2, v_tab_2, normf_w_2,
    )


_drawn_inputs = setup_inputs


def setup_inputs(seed=0):
    import zlib

    import numpy as np

    out = dict(_drawn_inputs(seed))
    spreads = {}
    factors = {'ssm_norm_w': 3.387,
     'ln_mix_post': 3.263,
     'ln_ffn_pre': 3.265,
     'ffn_conv_b': 3.165,
     'ln_ffn_post': 4.509,
     'w2_2': 8.0,
     'a0_2': 7.056,
     'k_k_2': 40.16,
     'k_a_2': 4.291,
     'lnx_w_2': 64.0,
     'lnx_b_2': 64.0,
     'q_norm_w_2': 42.263,
     'k_norm_w_2': 40.504,
     'norm1_w_2': 6.711,
     'norm2_w_2': 64.0,
     'normf_w_2': 7.74,
     'w_pq_2': 2.992,
     'sub_keys_2': 2.989,
     'u_tab_2': 3.533,
     'v_tab_2': 3.107}
    for name, (base, spread) in spreads.items():
        noise = np.random.default_rng([zlib.crc32(name.encode()), seed]).standard_normal(out[name].shape)
        drawn = base * np.exp(spread * noise) if base else spread * noise
        out[name] = jnp.asarray(drawn.astype(out[name].dtype))
    for name, factor in factors.items():
        out[name] = (out[name] * factor).astype(out[name].dtype)
    return out
```

```python
from contextlib import ExitStack

import numpy as np

import concourse.bass as bass
from concourse import mybir

F32 = mybir.dt.float32
F32R = mybir.dt.float32r
ACT = mybir.ActivationFunctionType
ALU = mybir.AluOpType
AX = mybir.AxisListType.X

P = 128
T = 256
TT = T // P
D = 2048
DT = D // P
PW = DT * P
HEADS1 = 8
SSM_H = 16
FFN_Q = 4
FQT = 11
EPS = 1e-6
NEG = -1e30

N_IN1 = 0
N_OUT1 = N_IN1 + 45
N_FFN = N_OUT1 + DT
FFN_STEP = 2 * FQT + DT
N_IN2 = N_FFN + FFN_Q * FFN_STEP
IN2 = 42
N_OUT2 = N_IN2 + IN2
N_PQ = N_OUT2 + DT
N_PEER = N_PQ + DT
PEER_G = 8
PEER_STEP = 2 * DT
N_END = N_PEER + PEER_G * PEER_STEP

S_XBC = 0
S_FFN = S_XBC + 12
S_IN2 = S_FFN + FFN_Q * FFN_STEP
S_PEER = S_IN2 + 30

PCOL = {}
_at = 0
for _name, _n in (
    ("ln_mix_pre", 16), ("ln_mix_post", 16), ("ln_ffn_pre", 16), ("ln_ffn_post", 16),
    ("ssm_conv_w", 48), ("ssm_conv_b", 12), ("ssm_norm_w", 8), ("d_skip", 8),
    ("ffn_conv_w", 264), ("ffn_conv_b", 88), ("dt_bias", 16), ("a_log", 16),
    ("mu_prev", 30), ("mu_next", 30), ("w0", 16), ("a0", 16), ("k_k", 8), ("k_a", 8), ("r_k", 8),
    ("lnx_w", 8), ("lnx_b", 8), ("q_norm", 1), ("k_norm", 1), ("norm1", 16), ("norm2", 16), ("normf", 16),
):
    PCOL[_name] = _at
    _at += _n
NPAR = _at

C_ID, C_ONES, C_CAUSAL, C_BUCKET = 0, 128, 256, 512
NCONST1 = 512 + 512
C2_BLOCK, C2_RESET, C2_PAIRS, C2_LEVELS, C2_EYE, C2_COS, C2_SIN, C2_PERM = (
    0, 128, 384, 640, 640 + 6 * 192, 640 + 6 * 192 + 64, 640 + 6 * 192 + 320, 640 + 6 * 192 + 576)
NCONST2 = C2_PERM + P

CH = 64
NCH = T // CH
LEVELS = 5
RWKV_SCALE = float(np.exp(-0.5))
GN_EPS = 64e-5


PEER_H = 8
K_TOP = 16
SLOTS = PEER_H * K_TOP
LOWEST = -3e38


def t5_buckets():
    n = np.maximum(256 - np.arange(512), 0)
    nf = np.maximum(n, 1).astype(np.float32)
    large = 16 + (np.log(nf / np.float32(16)) / np.float32(np.log(8.0)) * np.float32(16)).astype(np.int32)
    bucket = np.where(n < 16, n, np.minimum(large, 31))
    hot = np.zeros((P, 512), np.float32)
    hot[bucket, np.arange(512)] = 1.0
    hot[:32, 257:] = 0.0
    hot[32, 257:] = 1.0
    return hot


def consts1():
    row, col = np.arange(P)[:, None], np.arange(T)[None, :]
    c = np.zeros((P, NCONST1), np.float32)
    c[:, C_ID:C_ID + P] = np.eye(P)
    c[:, C_ONES:C_ONES + P] = 1.0
    c[:, C_CAUSAL:C_CAUSAL + T] = col >= row
    c[:, C_BUCKET:C_BUCKET + 512] = t5_buckets()
    return c



SQ = {"mix_pre": 0, "ssm": 4, "mix_post": 6, "ffn_pre": 10, "ffn_post": 14, "norm1": 18, "norm2": 22, "normf": 26}
RS = {"mix_pre": 0, "ssm": 1, "mix_post": 3, "ffn_pre": 4, "ffn_post": 5, "norm1": 6, "norm2": 7, "normf": 8}
HG = {"mix_pre": 0, "ssm": 4, "ffn_pre": 6, "norm1": 10, "norm2": 14}
XG = {"mix_post": 0, "ffn_post": 4, "mix2": 8, "peer": 12}


def consts2():
    row, col = np.arange(P)[:, None], np.arange(P)[None, :]
    c = np.zeros((P, NCONST2), np.float32)
    c[:, C2_BLOCK:C2_BLOCK + P] = row // 64 == col // 64
    c[:, C2_RESET:C2_RESET + T] = np.arange(T) % CH != 0
    s, t = row % CH, np.arange(CH)[None, :]
    for d, (strict, upto) in enumerate(((s < t, s <= t), (s > t, s >= t))):
        c[:, C2_PAIRS + P * d:C2_PAIRS + P * d + CH] = strict
        c[:, C2_PAIRS + P * d + CH:C2_PAIRS + P * (d + 1)] = upto
    t, s = row % CH, np.arange(CH)[None, :]
    for k in range(LEVELS + 1):
        n = 2 << k
        same = t // n == s // n
        forth = same & (s % n < n // 2) & (t % n >= n // 2)
        back = same & (t % n < n // 2) & (s % n >= n // 2)
        for d, m in enumerate((forth, back, forth)):
            c[:, C2_LEVELS + 192 * k + CH * d:C2_LEVELS + 192 * k + CH * (d + 1)] = m
    c[:, C2_EYE:C2_EYE + CH] = t == s
    token = np.arange(T)
    where = np.stack([token // 64, token % 64]).astype(np.float32)
    inv = (np.float32(10000.0) ** (-np.arange(0, 32, 2, dtype=np.float32) / np.float32(32))).astype(np.float32)
    d = np.arange(P) % 64
    angle = where[d // 32] * inv[d % 16][:, None]
    c[:, C2_COS:C2_COS + T] = np.cos(angle)
    c[:, C2_SIN:C2_SIN + T] = np.sin(angle)
    for o in range(P):
        if o % 32 < 16:
            c[o + 16, C2_PERM + o] = -1.0
        else:
            c[o - 16, C2_PERM + o] = 1.0
    return c


def consts3():
    return np.ascontiguousarray(np.broadcast_to(
        np.concatenate([np.arange(P), np.arange(K_TOP)]).astype(np.float32), (P, P + K_TOP)))


class Chain:

    def __init__(self, engine, semaphore, per, i=0):
        self.engine, self.semaphore, self.per, self.i, self.n = engine, semaphore, per, i, 0

    def step(self, instruction):
        instruction.then_inc(self.semaphore, 1)
        self.n += 1
        return self.n

    def wait(self, n):
        self.engine.wait_ge(self.semaphore, self.i * self.per + n)


def build(nc, a, out):
    with ExitStack() as ctx:
        def sb(name, shape, dt=F32, at=ctx):
            return at.enter_context(nc.sbuf_tensor(name, shape, dt))

        def sem(name):
            return ctx.enter_context(nc.semaphore(name))

        raw = [sb(f"raw{j}", [P, PW]) for j in range(2)]
        w_hi = [sb(f"w_hi{j}", [P, PW], F32R) for j in range(2)]
        w_lo = [sb(f"w_lo{j}", [P, PW], F32R) for j in range(2)]
        xT = sb("xT", [P, DT, T])
        h_hi = sb("h_hi", [P, DT, T], F32R)
        h_lo = sb("h_lo", [P, DT, T], F32R)
        par = sb("par", [P, NPAR])
        cst = sb("cst", [P, NCONST1])
        stage = [sb(f"stage{j}", [P, T]) for j in range(2)]
        quad = [sb(f"quad{j}", [P, 4, T]) for j in range(2)]
        rb = [sb(f"rb{j}", [P, T]) for j in range(2)]

        part = ExitStack()
        proj = sb("proj", [P, 44, T], at=part)
        bias = sb("bias", [P, HEADS1, T], at=part)
        v_nat = sb("v_nat", [P, TT, HEADS1 * P], at=part)
        logit = [sb(f"logit{j}", [P, T], at=part) for j in range(2)]
        prob = [sb(f"prob{j}", [P, T], at=part) for j in range(2)]
        prob_T = [sb(f"prob_T{j}", [P, TT, T], at=part) for j in range(2)]
        soft = sb("soft", [P, 4, 16], at=part)
        x_dt = sb("x_dt", [P, TT, SSM_H, 64], at=part)
        cb = sb("cb", [P, 2, 384], at=part)
        seg = [sb(f"seg{j}", [P, 384], at=part) for j in range(2)]
        mt = [sb(f"mt{j}", [P, 384], at=part) for j in range(2)]
        dt_T = sb("dt_T", [P, T], at=part)
        dts = sb("dts", [P, 9, TT * SSM_H], at=part)
        toep = [sb(f"toep{j}", [P, 512], at=part) for j in range(2)]
        relb = sb("relb", [64, HEADS1], at=part)
        part.close()
        acc = sb("acc", [P, DT, T], at=part)
        f_hi = sb("f_hi", [P, FQT, T], F32R, at=part)
        f_lo = sb("f_lo", [P, FQT, T], F32R, at=part)
        f_raw = sb("f_raw", [P, T], at=part)
        conv_g = sb("conv_g", [P, T], at=part)
        conv_u = sb("conv_u", [P, T], at=part)
        gelu_g = sb("gelu_g", [P, T], at=part)
        part.close()

        proj2 = sb("proj2", [P, IN2, T], at=part)
        cst2 = sb("cst2", [P, NCONST2], at=part)
        small2 = sb("small2", [P, 30 + 32 + 8 + 8], at=part)
        rwkv_at = ExitStack()
        k_swap = sb("k_swap", [P, 2, T], at=rwkv_at)
        v2_nat = sb("v2_nat", [P, TT, T], at=rwkv_at)
        prob2 = [sb(f"prob2_{j}", [P, TT, T], at=rwkv_at) for j in range(2)]
        prob2_T = [sb(f"prob2_T{j}", [P, TT, T], at=rwkv_at) for j in range(2)]
        soft2 = sb("soft2", [P, 4, 32], at=rwkv_at)
        q_ms = [sb(f"q_ms{j}", [P, 2, T], at=rwkv_at) for j in range(2)]
        q_rms = [sb(f"q_rms{j}", [P, 2, T], at=rwkv_at) for j in range(2)]
        rwkv_at.close()
        lora = sb("lora", [P, 6, P], at=rwkv_at)
        sig_w = sb("sig_w", [P, 2, T], at=rwkv_at)
        sig_a = sb("sig_a", [P, 2, T], at=rwkv_at)
        v_s = quad[1][:, 2, :]
        ar = sb("ar", [P, 2, 2, T], at=rwkv_at)
        bk = sb("bk", [P, 2, 2, T], at=rwkv_at)
        decay = sb("decay", [P, 2, T], at=rwkv_at)
        bk_nat = [sb(f"bk_nat{h}", [P, 8, CH], at=rwkv_at) for h in range(2)]
        uv = [sb(f"uv{h}", [P, 8, CH], at=rwkv_at) for h in range(2)]
        inv = sb("inv", [P, 8, CH], at=rwkv_at)
        inv_T = sb("inv_T", [P, 8, CH], at=rwkv_at)
        state = [sb(f"state{j}", [P, 2, CH], at=rwkv_at) for j in range(2)]
        state_w = sb("state_w", [P, 2, CH], at=rwkv_at)
        w_step = sb("w_step", [P, 2, CH], at=rwkv_at)
        pairs = [sb(f"pairs{h}", [P, 8, P], at=rwkv_at) for h in range(2)]
        n_T = proj2[:, 38:40, :].rearrange("p a (s t) -> p (a s) t", t=CH)
        t_one = proj2[:, 40:42, :].rearrange("p a (s t) -> p (a s) t", t=CH)
        lev = [quad[0][:, 2 * j:2 * j + 2, :].rearrange("p a (s t) -> p (a s) t", t=CH) for j in range(2)]
        rwkv_at.close()
        part.close()

        sb("acc_again", [P, DT, T], at=part)
        slot_T = sb("slot_T", [P, 3, T], at=part)
        count = sb("count", [P, P + K_TOP], at=part)
        hot_row = [sb(f"hot_row{j}", [P, 4, P], at=part) for j in range(2)]
        hot_col = [sb(f"hot_col{j}", [P, 4, P], at=part) for j in range(2)]
        top_at = ExitStack()
        sub_k = sb("sub_k", [P, 2 * PEER_H, P], at=top_at)
        cand = sb("cand", [P, PEER_H, K_TOP * K_TOP], at=top_at)
        hot = sb("hot", [P, SLOTS, K_TOP], at=top_at)
        rest = sb("rest", [P, PEER_H, T], at=top_at)
        top_v = sb("top_v", [P, TT, 2 * PEER_H, K_TOP], at=top_at)
        top_i = sb("top_i", [P, TT, 2 * PEER_H, K_TOP], mybir.dt.uint32, at=top_at)
        top_f = sb("top_f", [P, TT, 2 * PEER_H, K_TOP], at=top_at)
        best_v = sb("best_v", [P, TT, PEER_H, K_TOP], at=top_at)
        best_i = sb("best_i", [P, TT, PEER_H, K_TOP], mybir.dt.uint32, at=top_at)
        half_i = sb("half_i", [P, 2, TT, SLOTS], mybir.dt.uint32, at=top_at)
        half_f = sb("half_f", [P, 2, TT, SLOTS], at=top_at)
        slot = sb("slot", [P, 3, TT, SLOTS], at=top_at)
        gate_s = sb("gate_s", [P, 2, TT * PEER_H], at=top_at)
        top_at.close()
        g_stage = [sb(f"g_stage{j}", [P, PEER_G, 32, K_TOP], at=top_at) for j in range(2)]
        top_at.close()
        p_hi = sb("p_hi", [P, DT, T], F32R, at=top_at)
        p_lo = sb("p_lo", [P, DT, T], F32R, at=top_at)
        g_now = sb("g_now", [P, T, DT], at=top_at)
        p_raw = [sb(f"p_raw{j}", [P, T], at=top_at) for j in range(2)]
        top_at.close()
        part.close()
        gates_d = nc.dram_tensor("gates", (PEER_G, P, T, DT), F32, kind="Internal").ap()

        bank = [ctx.enter_context(nc.psum_tensor(f"bank{j}", [P, 512], F32)) for j in range(8)]
        toep_d = nc.dram_tensor("toeplitz", (HEADS1, P * 512 + 512), F32, kind="Internal").ap()

        s_par, s_cst, s_x = sem("par_loaded"), sem("cst_loaded"), sem("x_loaded")
        raw_loaded = [sem(f"raw_loaded{j}") for j in range(2)]
        hi_done, lo_done = sem("w_hi_done"), sem("w_lo_done")
        chunk_done = sem("chunk_done")
        copied = sem("copied")
        stage_used = sem("stage_used")
        sq_ready, sq_summed = sem("squares_ready"), sem("squares_summed")
        ms_done, rms_done, rstd_done = sem("ms_done"), sem("rms_done"), sem("rstd_done")
        quad_ready, h_hi_done, h_lo_done = sem("quad_ready"), sem("h_hi_done"), sem("h_lo_done")
        x_new, acc_done = sem("x_renewed"), sem("acc_scaled")
        relb_loaded, toep_done, toep_copied, bias_in = (
            sem("relb_loaded"), sem("toep_product"), sem("toep_copied"), sem("bias_loaded"))
        toep_out = [sem(f"toep_stored{j}") for j in range(2)]
        conv_step, pair_step, relb_set = sem("conv_step"), sem("pair_step"), sem("relb_set")
        vt_done, v_copied = sem("v_transposed"), sem("v_copied")
        score_done, logit_done, max_done, nmax_done = (
            sem("score_done"), sem("logit_done"), sem("max_done"), sem("nmax_done"))
        exp_done, rsum_done, prob_done = sem("exp_done"), sem("rsum_done"), sem("prob_done")
        pt_done, pt_copied, pv_done, mix_hi, mix_lo = (
            sem("probs_transposed"), sem("probs_copied"), sem("pv_done"), sem("mix_hi"), sem("mix_lo"))
        dt_tr, dt_step, dt_act, acs_done = sem("dt_transposed"), sem("dt_step"), sem("dt_act"), sem("acs_done")
        silu_done, xn_done, xdt_done = sem("silu_done"), sem("x_transposed"), sem("x_dt_done")
        cb_done, cb_masked = sem("cb_done"), sem("cb_masked")
        acsb_done, seg_done, decay_done, mt_done, y_done, y_read, y_gated = (
            sem("acsb_done"), sem("seg_done"), sem("decay_done"), sem("mt_done"), sem("y_done"),
            sem("y_read"), sem("y_gated"))
        gelu_done, f_raw_done, f_hi_done, f_lo_done = (
            sem("gelu_done"), sem("f_raw_done"), sem("f_hi_done"), sem("f_lo_done"))
        out_ready, out_stored = sem("out_ready"), [sem(f"out_stored{j}") for j in range(2)]
        sub_loaded, count_loaded, s3_done, acc_zero = (
            sem("sub_keys_loaded"), sem("count_loaded"), sem("scores3"), sem("acc_zero"))
        top_step, bank_read, best_ready, gate_exp, slots_done, slots_turned, turned_copied = (
            sem("top_step"), sem("scores3_read"), sem("best_less_max"), sem("gate_exp"), sem("slots_done"),
            sem("slots_transposed"), sem("slots_copied"))
        hot_ready, hot_used, gates_copied = sem("hot_ready"), sem("hot_used"), sem("gates_copied")
        gates_stored, g_loaded = [sem(f"gates_stored{j}") for j in range(2)], sem("gates_loaded")
        p_hi_done, p_lo_done = sem("p_hi_done"), sem("p_lo_done")
        cst2_loaded, prep2, shift_step = sem("cst2_loaded"), sem("prep2"), sem("shift_step")
        qk_sq, qk_sum, qk_ms, qk_rms, qk_inv, qk_norm, qk_turned, qk_step, qk_done = (
            sem("qk_squares"), sem("qk_summed"), sem("qk_ms"), sem("qk_rms"), sem("qk_inv"), sem("qk_normed"),
            sem("qk_turned"), sem("qk_step"), sem("qk_done"))
        k_swapped, v2_done, v2_copied = sem("k_swapped"), sem("v2_transposed"), sem("v2_copied")
        s2_done, max2_done, nmax2_done, exp2_done, rsum2_done, prob2_done = (
            sem("scores2"), sem("max2"), sem("nmax2"), sem("exp2"), sem("rsum2"), sem("probs2"))
        pt2_done, pt2_copied, pv2_done, mix2_hi, mix2_lo = (
            sem("probs2_transposed"), sem("probs2_copied"), sem("pv2"), sem("mix2_hi"), sem("mix2_lo"))
        kk_raw, kk_step, kk_done = sem("kk_raw"), sem("kk_step"), sem("kk_done")
        lora_act, lora_loaded, lora_used, tanh_done = (
            sem("lora_inputs"), sem("lora_loaded"), sem("lora_used"), sem("tanh_done"))
        rw_dve, expo_ready, expo_done, v_s_done, g_copied = (
            sem("rwkv_step"), sem("exponents"), sem("exps"), sem("v_s_done"), sem("g_copied"))
        vn_done, uv_v, rk_done, bonus_sum, scaled_done = (
            sem("v_chunks_transposed"), sem("v_chunks"), sem("r_k"), sem("bonus_sum"), sem("scaled"))
        n_done, nT_copied, lev_done, inv_start = sem("n_done"), sem("n_T_copied"), sem("level_masked"), sem("inv_start")
        t1_done, t1_copied, x_done, x_new2 = sem("t1_done"), sem("t1_copied"), sem("x_product"), sem("x_updated")
        bkn_done, bkn_copied, pairs_done, pairs_masked = (
            sem("bk_transposed"), sem("bk_copied"), sem("pairs_done"), sem("pairs_masked"))
        w_done, w_copied, u_done, u0_copied, u1_copied = (
            sem("w_done"), sem("w_copied"), sem("u_done"), sem("u0_copied"), sem("u1_copied"))
        st_scaled = sem("state_scaled")
        s_done, state_new, yy_done, yy_copied, rw_end = (
            sem("s_done"), sem("state_new"), sem("yy_done"), sem("yy_copied"), sem("rwkv_round"))
        gn_mean, gn_centred, gn_step, gn_out, gn_hi = (
            sem("gn_mean"), sem("gn_centred"), sem("gn_step"), sem("gn_out"), sem("gn_hi"))
        HEAD_KK, HEAD_GN = 5, 9

        def pc(name, i=0, n=1):
            return par[:, PCOL[name] + i:PCOL[name] + i + n]

        ident = cst[:, C_ID:C_ID + P]
        ones = cst[:, C_ONES:C_ONES + P]
        causal = cst[:, C_CAUSAL:C_CAUSAL + T]

        blk = cst2[:, C2_BLOCK:C2_BLOCK + P]
        eye = cst2[:, C2_EYE:C2_EYE + CH]
        reset = cst2[:, C2_RESET:C2_RESET + T]
        shift_c, half_w, omka, half_rk = (
            small2[:, 0:30], small2[:, 30:62], small2[:, 62:70], small2[:, 70:78])

        def tile_of(t, i):
            if isinstance(i, int):
                return t[:, i, :]
            return t[:, bass.ds(i, 1), :].rearrange("p a n -> p (a n)")

        def twice(t, i):
            return t[:, bass.ds(i, 1), :].to_broadcast([P, 2, T])

        def chunk_of(i, d):
            return i if d == 0 else NCH - 1 - i

        block = ctx.enter_context(nc.Block())

        @block.sync
        def _(sp):
            def load(arr, c, it, i, width=PW):
                if c >= 2 or not isinstance(it, int):
                    sp.wait_ge(lo_done, it * 2 + (c - 1))
                sp.dma_start(raw[c % 2][:, 0:width], arr[bass.ds(i, 1)].rearrange("a p n -> (a p) n")
                             ).then_inc(raw_loaded[c % 2], 16)

            def loads(arr, n0, count, width=PW):
                with sp.Fori(0, count // 2) as i:
                    for j in range(2):
                        load(arr, n0 + j, i, i * 2 + j, width)

            sp.dma_start(cst[:], a["consts1"]).then_inc(s_cst, 16)
            for g in range(4):
                sp.dma_start(xT[:, 4 * g:4 * g + 4, :], a["x"][:, 4 * g:4 * g + 4, :]).then_inc(s_x, 16)
            load(a["w_in1"], 0, 0, 0)
            sp.dma_start(par[:], a["params"]).then_inc(s_par, 16)
            sp.dma_start(relb[0:32, :], a["rel_bias"]).then_inc(relb_loaded, 16)
            load(a["w_in1"], 1, 0, 1)
            with sp.Fori(1, 22) as i:
                for j in range(2):
                    load(a["w_in1"], j, i, i * 2 + j)
            load(a["w_in1"], 44, 0, 44)
            loads(a["w_out1"], N_OUT1, DT)
            with sp.Fori(0, FFN_Q) as q:
                with sp.Fori(0, FQT) as i:
                    for j in range(2):
                        load(a["w_up"], N_FFN + j, q * (FFN_STEP // 2) + i, q * (2 * FQT) + i * 2 + j)
                with sp.Fori(0, DT // 2) as i:
                    for j in range(2):
                        load(a["w_down"], N_FFN + 2 * FQT + j, q * (FFN_STEP // 2) + i, q * DT + i * 2 + j, FQT * P)
            sp.wait_ge(h_lo_done, HG["ffn_pre"] + 4)
            sp.dma_start(cst2[:], a["consts2"]).then_inc(cst2_loaded, 16)
            loads(a["w_in2"], N_IN2, IN2)
            for j in range(2):
                load(a["w_out2"], N_OUT2 + j, 0, j)
            with sp.Fori(0, 8) as m:
                sp.wait_ge(lora_used, m + 1)
                sp.dma_start(lora[:], a["lora"][bass.ds(m, 1)].rearrange("a p k n -> (a p) k n")
                             ).then_inc(lora_loaded, 16)
            with sp.Fori(1, DT // 2) as i:
                for j in range(2):
                    load(a["w_out2"], N_OUT2 + j, i, i * 2 + j)
            for j in range(2):
                load(a["w_pq"], N_PQ + j, 0, j)
            sp.wait_ge(h_lo_done, HG["norm2"] + 4)
            sp.dma_start(sub_k[:], a["sub_keys"]).then_inc(sub_loaded, 16)
            sp.dma_start(count[:], a["consts3"]).then_inc(count_loaded, 16)
            with sp.Fori(1, DT // 2) as i:
                for j in range(2):
                    load(a["w_pq"], N_PQ + j, i, i * 2 + j)
            with sp.Fori(0, PEER_G) as g:
                with sp.Fori(0, DT // 2) as i:
                    for j in range(2):
                        load(a["u_tab"], N_PEER + j, g * DT + i, g * DT + i * 2 + j)
                with sp.Fori(0, DT // 2) as i:
                    for j in range(2):
                        load(a["v_tab"], N_PEER + DT + j, g * DT + i, g * DT + i * 2 + j)
            for g in range(4):
                sp.wait_ge(out_ready, g + 1)
                sp.dma_start(out[:, 4 * g:4 * g + 4, :], quad[g % 2][:]).then_inc(out_stored[g % 2], 16)
            for j in range(2):
                sp.wait_ge(out_stored[j], 32)

        @block.tensor
        def _(pe):
            def chunk(c, it, hi, lo, nk=DT, per_tile=None):
                n = it * 2 + c
                pe.wait_ge(lo_done, n + 1)
                if c >= 2 or not isinstance(it, int):
                    pe.wait_ge(copied, n - 1)
                o = bank[c % 2][:, 0:T]
                for k in range(nk):
                    if per_tile:
                        per_tile(k)
                    wh, wl = w_hi[c % 2][:, k * P:(k + 1) * P], w_lo[c % 2][:, k * P:(k + 1) * P]
                    nc.tensor.matmul(o, wh, hi[:, k, :], start=(k == 0), stop=False)
                    nc.tensor.matmul(o, wh, lo[:, k, :], start=False, stop=False)
                    last = nc.tensor.matmul(o, wl, hi[:, k, :], start=False, stop=(k == nk - 1))
                last.then_inc(chunk_done, 1)

            def chunks(n0, count, hi, lo, nk=DT, per_tile=None):
                with pe.Fori(0, count // 2) as i:
                    for j in range(2):
                        chunk(n0 + j, i, hi, lo, nk, per_tile if j == 0 else None)

            def normed_by(first):
                def per_tile(k):
                    if k % 4 == 0:
                        pe.wait_ge(h_lo_done, first + k // 4 + 1)
                return per_tile

            def sums(first, groups):
                for g in range(groups):
                    pe.wait_ge(sq_ready, first + g + 1)
                    for k in range(4):
                        last = nc.tensor.matmul(bank[2][:, 0:T], ones, quad[g % 2][:, k, :],
                                                start=(g == 0 and k == 0), stop=(g == groups - 1 and k == 3))
                    last.then_inc(sq_summed, 1)

            pe.wait_ge(s_cst, 16)
            sums(SQ["mix_pre"], 4)
            pe.wait_ge(relb_loaded, 16)
            pe.wait_ge(relb_set, 1)
            for h in range(HEADS1):
                if h >= 2:
                    pe.wait_ge(toep_copied, h - 1)
                nc.tensor.matmul(bank[3 + h % 2][:], relb[0:33, h:h + 1].to_broadcast([33, P]),
                                 cst[0:33, C_BUCKET:C_BUCKET + 512], start=True, stop=True).then_inc(toep_done, 1)
            for c in range(2):
                chunk(c, 0, h_hi, h_lo, per_tile=normed_by(HG["mix_pre"]) if c == 0 else None)
            with pe.Fori(1, 22) as i:
                for j in range(2):
                    chunk(j, i, h_hi, h_lo)
            chunk(44, 0, h_hi, h_lo)

            pe.wait_ge(copied, 45)
            for st in range(TT):
                for half in range(2):
                    u = 2 * st + half
                    if u == 0:
                        pe.wait_ge(toep_copied, HEADS1)
                    if u >= 2:
                        pe.wait_ge(v_copied, u - 1)
                    for k in range(4):
                        last = nc.tensor.transpose(bank[3 + u % 2][:, k * P:(k + 1) * P],
                                                   proj[:, 16 + 4 * half + k, st * P:(st + 1) * P], ident)
                    last.then_inc(vt_done, 1)

            def scores(u):
                h, i = u // 2, u % 2
                pe.wait_ge(v_copied, 4)
                if u >= 2:
                    pe.wait_ge(logit_done, u - 1)
                nc.tensor.matmul(bank[3 + i][:, 0:(i + 1) * P], proj[:, h, i * P:(i + 1) * P],
                                 proj[:, 8 + h, 0:(i + 1) * P], start=True, stop=True).then_inc(score_done, 1)

            scores(0)
            scores(1)
            for u in range(2 * HEADS1):
                h, i = u // 2, u % 2
                if u + 2 < 2 * HEADS1:
                    scores(u + 2)
                pe.wait_ge(prob_done, u + 1)
                if u >= 2:
                    pe.wait_ge(pt_copied, u - 1)
                for st in range(i + 1):
                    last = nc.tensor.transpose(bank[5 + i][:, st * P:(st + 1) * P],
                                               prob[i][:, st * P:(st + 1) * P], ident)
                last.then_inc(pt_done, 1)
                if i:
                    pe.wait_ge(pt_copied, u + 1)
                    if h:
                        pe.wait_ge(mix_lo, h)
                    nc.tensor.matmul(bank[7][:, 0:T], v_nat[:, 0, h * P:(h + 1) * P], prob_T[h % 2][:, 0, :],
                                     start=True, stop=False)
                    nc.tensor.matmul(bank[7][:, P:T], v_nat[:, 1, h * P:(h + 1) * P], prob_T[h % 2][:, 1, P:T],
                                     start=False, stop=True).then_inc(pv_done, 1)

            for st in range(TT):
                last = nc.tensor.transpose(bank[3][:, st * SSM_H:(st + 1) * SSM_H],
                                           dt_T[0:SSM_H, st * P:(st + 1) * P], ident[0:SSM_H, 0:SSM_H])
            last.then_inc(dt_tr, 1)
            dta = dts[:, 7, :]
            pe.wait_ge(dt_step, 12)
            nc.tensor.matmul(bank[4][:, 0:16], causal[:, 0:P], dta[:, 0:16], start=True, stop=True)
            nc.tensor.matmul(bank[4][:, 16:32], causal[:, P:T], dta[:, 0:16], start=True, stop=False)
            nc.tensor.matmul(bank[4][:, 16:32], causal[:, 0:P], dta[:, 16:32], start=False,
                             stop=True).then_inc(acs_done, 1)

            pe.wait_ge(silu_done, 3)
            for u in range(4):
                st, half = u // 2, u % 2
                if u == 0:
                    pe.wait_ge(pt_copied, 2 * HEADS1)
                if u >= 2:
                    pe.wait_ge(xdt_done, u - 1)
                for k in range(4):
                    last = nc.tensor.transpose(bank[5 + u % 2][:, k * P:(k + 1) * P],
                                               proj[:, 32 + 4 * half + k, st * P:(st + 1) * P], ident)
                last.then_inc(xn_done, 1)
            for g in range(2):
                if g == 0:
                    pe.wait_ge(mix_lo, HEADS1)
                else:
                    pe.wait_ge(cb_masked, 2)
                b_t, c_t = proj[:, 40 + g, :], proj[:, 42 + g, :]
                nc.tensor.matmul(bank[7][:, 0:T], b_t[:, 0:P], c_t, start=True, stop=True)
                nc.tensor.matmul(bank[7][:, T:T + P], b_t[:, P:T], c_t[:, P:T],
                                 start=True, stop=True).then_inc(cb_done, 1)
            def acs_rows(h):
                if h < 2:
                    pe.wait_ge(dt_step, 13)
                else:
                    pe.wait_ge(seg_done, h - 1)
                nc.tensor.matmul(bank[3 + h % 2][:, 0:T], dta[:, h:h + 1].to_broadcast([P, P]), causal,
                                 start=True, stop=False)
                nc.tensor.matmul(bank[3 + h % 2][:, P:T], dta[:, 16 + h:17 + h].to_broadcast([P, P]),
                                 causal[:, 0:P], start=False, stop=True).then_inc(acsb_done, 1)

            pe.wait_ge(xdt_done, 4)
            acs_rows(0)
            acs_rows(1)
            for h in range(SSM_H):
                if h + 2 < SSM_H:
                    acs_rows(h + 2)
                pe.wait_ge(mt_done, h + 1)
                m, r = h // 2, (h % 2) * 64
                if m >= 2:
                    pe.wait_ge(y_read, m - 1)
                o = bank[5 + m % 2]
                nc.tensor.matmul(o[r:r + 64, 0:T], x_dt[:, 0, h, :], mt[h % 2][:, 0:T], start=True, stop=False)
                nc.tensor.matmul(o[r:r + 64, P:T], x_dt[:, 1, h, :], mt[h % 2][:, T:T + P],
                                 start=False, stop=True).then_inc(y_done, 1)
            for g in range(2):
                pe.wait_ge(sq_ready, SQ["ssm"] + g + 1)
                if g == 1:
                    pe.wait_ge(ms_done, RS["ssm"] + 1)
                for k in range(4):
                    last = nc.tensor.matmul(bank[2][:, 0:T], ones, quad[g][:, k, :], start=(k == 0), stop=(k == 3))
                last.then_inc(sq_summed, 1)
            def mixed(k):
                if k in (8, 12):
                    pe.wait_ge(h_lo_done, HG["ssm"] + (k - 4) // 4)
            chunks(N_OUT1, DT, h_hi, h_lo, per_tile=mixed)
            sums(SQ["mix_post"], 4)
            sums(SQ["ffn_pre"], 4)
            with pe.Fori(0, FFN_Q) as q:
                with pe.Fori(0, FQT) as i:
                    for j in range(2):
                        chunk(N_FFN + j, q * (FFN_STEP // 2) + i, h_hi, h_lo,
                              per_tile=normed_by(HG["ffn_pre"]) if j == 0 else None)
                n0 = N_FFN + 2 * FQT

                def f_ready(k):
                    if k == 0:
                        pe.wait_ge(f_lo_done, q * FQT + (FQT - 1))
                    if k == FQT - 1:
                        pe.wait_ge(f_lo_done, q * FQT + FQT)
                chunk(n0, q * (FFN_STEP // 2), f_hi, f_lo, FQT, f_ready)
                chunk(n0 + 1, q * (FFN_STEP // 2), f_hi, f_lo, FQT)
                with pe.Fori(1, DT // 2) as i:
                    for j in range(2):
                        chunk(n0 + j, q * (FFN_STEP // 2) + i, f_hi, f_lo, FQT)
            sums(SQ["ffn_post"], 4)
            sums(SQ["norm1"], 4)
            chunks(N_IN2, IN2, h_hi, h_lo, per_tile=normed_by(HG["norm1"]))

            pe.wait_ge(cst2_loaded, 16)
            for p in range(6):
                if p < 5:
                    pe.wait_ge(qk_sq, p + 1)
                    if p >= 2:
                        pe.wait_ge(qk_ms, p - 1)
                    nc.tensor.matmul(bank[3 + p % 2][:], blk, quad[p % 2][:, 0:2, :], start=True, stop=True
                                     ).then_inc(qk_sum, 1)
                if p:
                    u = p - 1
                    pe.wait_ge(qk_norm, u + 1)
                    if u >= 2:
                        pe.wait_ge(qk_done, u - 1)
                    nc.tensor.matmul(bank[5 + u % 2][:], cst2[:, C2_PERM:C2_PERM + P],
                                     proj2[:, 30 + 2 * u:32 + 2 * u, :], start=True, stop=True
                                     ).then_inc(qk_turned, 1)
            for st in range(TT):
                for k in range(2):
                    last = nc.tensor.transpose(bank[7][:, st * T + k * P:st * T + (k + 1) * P],
                                               proj2[:, 40 + k, st * P:(st + 1) * P], ident)
            last.then_inc(v2_done, 1)

            def scores2(qh):
                m, r, g = qh // 2, (qh % 2) * 64, qh // 4
                if qh == 0:
                    pe.wait_ge(qk_done, 5)
                    pe.wait_ge(k_swapped, 32)
                if qh >= 2:
                    pe.wait_ge(exp2_done, 2 * (qh - 1))
                k_t = proj2[r:r + 64, 38 + g // 2, :] if g % 2 == qh % 2 else k_swap[r:r + 64, g // 2, :]
                for tt in range(TT):
                    last = nc.tensor.matmul(bank[3 + qh % 2][:, tt * T:(tt + 1) * T],
                                            proj2[r:r + 64, 30 + m, tt * P:(tt + 1) * P], k_t,
                                            start=True, stop=True)
                last.then_inc(s2_done, 1)

            scores2(0)
            scores2(1)
            for qh in range(16):
                m, r, g = qh // 2, (qh % 2) * 64, qh // 4
                if qh + 2 < 16:
                    scores2(qh + 2)
                pe.wait_ge(prob2_done, qh + 1)
                if qh >= 2:
                    pe.wait_ge(pt2_copied, qh - 1)
                for st in range(TT):
                    for tt in range(TT):
                        last = nc.tensor.transpose(bank[5 + qh % 2][:, st * T + tt * P:st * T + (tt + 1) * P],
                                                   prob2[qh % 2][:, tt, st * P:(st + 1) * P], ident)
                last.then_inc(pt2_done, 1)
                pe.wait_ge(pt2_copied, qh + 1)
                if qh == 0:
                    pe.wait_ge(v2_copied, 1)
                if m >= 2:
                    pe.wait_ge(mix2_lo, m - 1)
                o = bank[7 if m % 2 else 2][r:r + 64, 0:T]
                for st in range(TT):
                    last = nc.tensor.matmul(o, v2_nat[:, st, g * 64:(g + 1) * 64], prob2_T[qh % 2][:, st, :],
                                            start=(st == 0), stop=(st == TT - 1))
                last.then_inc(pv2_done, 1)

            for p in range(4):
                pe.wait_ge(qk_sq, HEAD_KK + p + 1)
                if p >= 2:
                    pe.wait_ge(qk_rms, HEAD_KK + p - 1)
                nc.tensor.matmul(bank[3 + p % 2][:], blk, quad[p % 2][:, 0:2, :], start=True, stop=True
                                 ).then_inc(qk_sum, 1)
            def small(o, lhs, rhs, stop=True, start=True):
                return nc.tensor.matmul(o, lhs, rhs, start=start, stop=stop)

            def counts_first(*counts):
                for c in counts:
                    pe.to_reg(c)
                pe.wait_ge(s_cst, 16)

            pe.wait_ge(lora_act, 2)
            with pe.Fori(0, 8) as m:
                pe.wait_ge(rw_end, m + 1)
                pe.wait_ge(lora_loaded, m * 16 + 16)
                for d in range(2):
                    nc.tensor.matmul(bank[3][:, d * T:(d + 1) * T], lora[0:96, d, :], proj2[0:96, 24 + d, :],
                                     start=True, stop=True)
                    nc.tensor.matmul(bank[4][:, d * T:(d + 1) * T], lora[0:96, 2 + d, :], proj2[0:96, 26 + d, :],
                                     start=True, stop=True)
                for k in range(2):
                    last = nc.tensor.matmul(bank[5][:, 0:T], lora[:, 4 + k, :], proj2[:, 28 + k, :],
                                            start=(k == 0), stop=(k == 1))
                last.then_inc(lora_used, 1)
                counts_first(m + 1)
                pe.wait_ge(v_s_done, m + 1)
                for i in range(NCH):
                    for d in range(2):
                        for r in (0, 64):
                            c = chunk_of(i, d)
                            last = small(bank[6][r:r + 64, (2 * i + d) * CH:(2 * i + d + 1) * CH],
                                           v_s[r:r + 64, c * CH:(c + 1) * CH], eye[r:r + 64, :])
                last.then_inc(vn_done, 1)
                pe.wait_ge(rk_done, m + 1)
                nc.tensor.matmul(bank[7][:, 0:T], blk, quad[1][:, 3, :], start=True, stop=True
                                 ).then_inc(bonus_sum, 1)
                counts_first(m + 1)
                pe.wait_ge(scaled_done, m + 1)

                for i in range(NCH):
                    for d in range(2):
                        for r in (0, 64):
                            c, s = chunk_of(i, d) * CH, (2 * i + d) * CH
                            a_t, b_t = ar[r:r + 64, 0, d, c:c + CH], bk[r:r + 64, 0, d, c:c + CH]
                            small(bank[3][r:r + 64, s:s + CH], a_t, b_t)
                            last = small(bank[4][r:r + 64, s:s + CH], b_t, a_t)
                last.then_inc(n_done, 1)

                def by_token():
                    for i in range(NCH):
                        for d in range(2):
                            c, s = chunk_of(i, d) * CH, (2 * i + d) * CH
                            for h in range(2):
                                r = 64 * h
                                small(bank[h][r:r + 64, s:s + CH], bk[r:r + 64, 1, d, c:c + CH], eye[r:r + 64, :])
                            for h in range(2):
                                r = 64 * h
                                last = small(bank[h][64 - r:128 - r, s:s + CH], bk[r:r + 64, 0, d, c:c + CH],
                                             eye[r:r + 64, :])
                    last.then_inc(bkn_done, 2)

                def pair_products(h, half, o):
                    r = 64 * h
                    for x in range(4):
                        i, d = 2 * half + x // 2, x % 2
                        c = chunk_of(i, d) * CH
                        rhs = ar[r:r + 64, :, d, c:c + CH]
                        small(o[r:r + 64, x * P:(x + 1) * P], bk[r:r + 64, 1, d, c:c + CH], rhs)
                        last = small(o[64 - r:128 - r, x * P:(x + 1) * P], bk[r:r + 64, 0, d, c:c + CH], rhs)
                    last.then_inc(pairs_done, 1)

                for k in range(1, LEVELS + 1):
                    counts_first(m * LEVELS + k, m * (LEVELS + 1) + k)
                    pe.wait_ge(lev_done, m * LEVELS + k)
                    pe.wait_ge(x_new2, m * (LEVELS + 1) + k)
                    for s in range(8):
                        for r in (0, 64):
                            last = small(bank[5][r:r + 64, s * CH:(s + 1) * CH], lev[k % 2][r:r + 64, s, :],
                                           inv[r:r + 64, s, :])
                    last.then_inc(t1_done, 1)
                    if k == 1:
                        by_token()
                    elif k == 2:
                        pair_products(0, 0, bank[2])
                    elif k == 3:
                        pair_products(1, 0, bank[3])
                    elif k == 4:
                        pair_products(0, 1, bank[4])
                    else:
                        counts_first(m * 2 + 2)
                        pe.wait_ge(bkn_copied, m * 2 + 2)
                        pair_products(1, 1, bank[0])
                    counts_first(m * LEVELS + k)
                    pe.wait_ge(t1_copied, m * LEVELS + k)
                    for s in range(8):
                        for r in (0, 64):
                            last = small(bank[7][r:r + 64, s * CH:(s + 1) * CH], t_one[r:r + 64, s, :],
                                           inv_T[r:r + 64, s, :])
                            if k < LEVELS:
                                last = small(bank[6][r:r + 64, s * CH:(s + 1) * CH], inv_T[r:r + 64, s, :],
                                             t_one[r:r + 64, s, :])
                    last.then_inc(x_done, 1)
                counts_first(m * (LEVELS + 1) + LEVELS + 1, m * 4 + 4, m * 2 + 2)
                pe.wait_ge(x_new2, m * (LEVELS + 1) + LEVELS + 1)
                pe.wait_ge(pairs_masked, m * 4 + 4)
                pe.wait_ge(uv_v, m * 2 + 2)
                pe.wait_ge(bkn_copied, m * 2 + 2)
                for i in range(NCH):
                    counts_first(m * NCH + i + 1)
                    pe.wait_ge(state_new, m * NCH + i + 1)
                    st = state[i % 2]
                    for d in range(2):
                        c, s = chunk_of(i, d) * CH, 2 * i + d
                        for h in range(2):
                            r = 64 * h
                            small(bank[5][r:r + 64, d * CH:(d + 1) * CH], ar[r:r + 64, 0, d, c:c + CH],
                                  st[r:r + 64, d, :], stop=False)
                        for h in range(2):
                            r = 64 * h
                            last = small(bank[5][r:r + 64, d * CH:(d + 1) * CH], pairs[h][r:r + 64, s, 0:CH],
                                         uv[h][r:r + 64, s, :], start=False)
                    last.then_inc(w_done, 1)
                    counts_first(m * NCH + i + 1)
                    pe.wait_ge(w_copied, m * NCH + i + 1)
                    for d in range(2):
                        for r in (0, 64):
                            last = small(bank[6][64 - r:128 - r, d * CH:(d + 1) * CH],
                                           inv_T[r:r + 64, 2 * i + d, :], w_step[r:r + 64, d, :])
                    last.then_inc(u_done, 1)
                    counts_first(m * NCH + i + 1)
                    pe.wait_ge(u0_copied, m * NCH + i + 1)
                    pe.wait_ge(u1_copied, m * NCH + i + 1)
                    if i < NCH - 1:
                        for h in range(2):
                            for d in range(2):
                                last = small(bank[7][64 * h:64 * h + 64, d * CH:(d + 1) * CH],
                                             bk_nat[h][:, 2 * i + d, :], uv[h][:, 2 * i + d, :])
                        last.then_inc(s_done, 1)
                    if i:
                        counts_first(m * (2 * NCH) + 2 * i)
                        pe.wait_ge(yy_copied, m * (2 * NCH) + 2 * i)
                    for h in range(2):
                        r = 64 * h
                        for d in range(2):
                            c, s = chunk_of(i, d) * CH, 2 * i + d
                            o = bank[1][r:r + 64, d * CH:(d + 1) * CH]
                            small(o, st[r:r + 64, d, :], ar[r:r + 64, 1, d, c:c + CH], stop=False)
                            last = small(o, uv[h][:, s, :], pairs[h][:, s, CH:P], start=False)
                    last.then_inc(yy_done, 1)
            pe.wait_ge(rw_end, 9)
            for p in range(5):
                if p < 4:
                    if p >= 2:
                        pe.wait_ge(gn_centred, p - 1)
                    nc.tensor.matmul(bank[3 + p % 2][:], blk, proj2[:, 2 * p:2 * p + 2, :], start=True, stop=True
                                     ).then_inc(gn_mean, 1)
                if p:
                    u = p - 1
                    pe.wait_ge(qk_sq, HEAD_GN + u + 1)
                    if u >= 2:
                        pe.wait_ge(qk_ms, 5 + u - 1)
                    nc.tensor.matmul(bank[5 + u % 2][:], blk, quad[u % 2][:, 0:2, :], start=True, stop=True
                                     ).then_inc(qk_sum, 1)
            def mixed2(k):
                if k < 8 and k % 2 == 0:
                    pe.wait_ge(mix2_lo, 8 + k // 2 + 1)
            chunks(N_OUT2, DT, h_hi, h_lo, per_tile=mixed2)
            sums(SQ["norm2"], 4)
            chunks(N_PQ, DT, h_hi, h_lo, per_tile=normed_by(HG["norm2"]))

            pe.wait_ge(copied, N_PQ + DT)
            pe.wait_ge(sub_loaded, 16)
            for u in range(8):
                tt, grp = u // 4, u % 4
                if u >= 2:
                    pe.wait_ge(bank_read, u - 1)
                for x in range(4):
                    last = nc.tensor.matmul(bank[3 + u % 2][:, x * P:(x + 1) * P],
                                            acc[:, 4 * grp + x, tt * P:(tt + 1) * P], sub_k[:, 4 * grp + x, :],
                                            start=True, stop=True)
                last.then_inc(s3_done, 1)
            pe.wait_ge(slots_done, 1)
            for x in range(3):
                for tt in range(TT):
                    u = x * TT + tt
                    last = nc.tensor.transpose(bank[5 + u // 4][:, (u % 4) * P:(u % 4 + 1) * P],
                                               slot[:, x, tt, :], ident)
                    if u % 4 == 3 or u == 5:
                        last.then_inc(slots_turned, 1)
            pe.wait_ge(turned_copied, 2)
            def gates(i, j, first=False):
                pe.wait_ge(hot_ready, i * 2 + (j + 1))
                if not first:
                    pe.wait_ge(gates_copied, i * 2 + (j - 1))
                for x in range(4):
                    last = nc.tensor.matmul(bank[3 + j][:, x * P:(x + 1) * P], hot_col[j][:, x, :],
                                            hot_row[j][:, x, :], start=True, stop=True)
                last.then_inc(hot_used, 1)

            for j in range(2):
                gates(0, j, first=True)
            with pe.Fori(1, T // 8) as i:
                for j in range(2):
                    gates(i, j)
            with pe.Fori(0, PEER_G) as g:
                with pe.Fori(0, DT // 2) as i:
                    for j in range(2):
                        chunk(N_PEER + j, g * DT + i, h_hi, h_lo)

                def p_ready(k):
                    if k == 0:
                        pe.wait_ge(p_lo_done, g * DT + (DT - 1))
                    if k == DT - 1:
                        pe.wait_ge(p_lo_done, g * DT + DT)
                chunk(N_PEER + DT, g * DT, p_hi, p_lo, DT, p_ready)
                chunk(N_PEER + DT + 1, g * DT, p_hi, p_lo)
                with pe.Fori(1, DT // 2) as i:
                    for j in range(2):
                        chunk(N_PEER + DT + j, g * DT + i, p_hi, p_lo)
            sums(SQ["normf"], 4)

        @block.scalar
        def _(act):
            def split(c, it):
                act.wait_ge(raw_loaded[c % 2], it * 16 + (c // 2 + 1) * 16)
                if c >= 2 or not isinstance(it, int):
                    act.wait_ge(chunk_done, it * 2 + (c - 1))
                nc.scalar.activation(w_hi[c % 2][:], raw[c % 2][:], ACT.Copy).then_inc(hi_done, 1)

            def copy(c, it, dst, func=ACT.Copy):
                act.wait_ge(chunk_done, it * 2 + (c + 1))
                nc.scalar.activation(dst, bank[c % 2][:, 0:T], func).then_inc(copied, 1)

            def to_stage(c, it, s, s_it, func=ACT.Copy):
                if s >= 2 or not isinstance(s_it, int):
                    act.wait_ge(stage_used, s_it * 2 + (s - 1))
                copy(c, it, stage[s % 2][:], func)

            def plain(n0, count, dst, d0=0):
                with act.Fori(0, count // 2) as i:
                    for j in range(2):
                        copy(n0 + j, i, dst[:, bass.ds(i * 2 + (d0 + j), 1), :].rearrange("p a n -> p (a n)"))
                        split(n0 + j + 2, i)

            def squares(src, first, ready, groups=4):
                for g in range(groups):
                    ready(g)
                    if g >= 2:
                        act.wait_ge(sq_summed, first + g - 1)
                    nc.scalar.activation(quad[g % 2][:], src[:, 4 * g:4 * g + 4, :], ACT.Square
                                         ).then_inc(sq_ready, 1)

            def rms(i):
                act.wait_ge(ms_done, i + 1)
                nc.scalar.activation(rb[1][:], rb[0][:], ACT.Sqrt).then_inc(rms_done, 1)

            def h_upper(first, groups=4, tile0=0):
                for g in range(groups):
                    act.wait_ge(quad_ready, first + g + 1)
                    nc.scalar.activation(h_hi[:, tile0 + 4 * g:tile0 + 4 * g + 4, :], quad[g % 2][:], ACT.Copy
                                         ).then_inc(h_hi_done, 1)

            squares(xT, SQ["mix_pre"], lambda g: act.wait_ge(s_x, 64))
            split(0, 0)
            rms(RS["mix_pre"])
            h_upper(HG["mix_pre"])
            split(1, 0)
            for h in range(HEADS1):
                act.wait_ge(toep_done, h + 1)
                if h >= 2:
                    act.wait_ge(toep_out[h % 2], 16 * (h // 2))
                nc.scalar.activation(toep[h % 2][:], bank[3 + h % 2][:], ACT.Copy).then_inc(toep_copied, 1)
            plain(0, 32, proj)
            for j in range(2):
                to_stage(32 + j, 0, j, 0)
                split(34 + j, 0)
            with act.Fori(1, 6) as i:
                for j in range(2):
                    to_stage(32 + j, i, j, i)
                    split(34 + j, i)
            copy(44, 0, dt_T[:])
            split(46, 0)

            for u in range(4):
                act.wait_ge(vt_done, u + 1)
                nc.scalar.activation(v_nat[:, u // 2, (u % 2) * 512:(u % 2) * 512 + 512], bank[3 + u % 2][:],
                                     ACT.Copy).then_inc(v_copied, 1)
            for u in range(2 * HEADS1):
                h, i = u // 2, u % 2
                w = (i + 1) * P
                act.wait_ge(nmax_done, u + 1)
                if u >= 2:
                    act.wait_ge(pt_done, u - 1)
                nc.scalar.activation(prob[i][:, 0:w], logit[i][:, 0:w], ACT.Exp, bias=soft[:, 0, u:u + 1],
                                     accum_out=soft[:, 1, u:u + 1]).then_inc(exp_done, 1)
                act.wait_ge(pt_done, u + 1)
                if h >= 2 and i == 0:
                    act.wait_ge(pv_done, h - 1)
                nc.scalar.activation(prob_T[h % 2][:, 0:i + 1, i * P:(i + 1) * P],
                                     bank[5 + i][:, 0:w].rearrange("p (s t) -> p s t", t=P), ACT.Copy
                                     ).then_inc(pt_copied, 1)
                if i:
                    act.wait_ge(pv_done, h + 1)
                    nc.scalar.activation(h_hi[:, h, :], bank[7][:, 0:T], ACT.Copy).then_inc(mix_hi, 1)

            act.wait_ge(stage_used, 12)
            for g in range(3):
                nc.scalar.activation(proj[:, 32 + 4 * g:36 + 4 * g, :], proj[:, 32 + 4 * g:36 + 4 * g, :], ACT.Silu
                                     ).then_inc(silu_done, 1)
            for g in range(2):
                nc.scalar.activation(proj[:, 24 + 4 * g:28 + 4 * g, :], proj[:, 24 + 4 * g:28 + 4 * g, :], ACT.Silu
                                     ).then_inc(silu_done, 1)
            act.wait_ge(dt_step, 3)
            nc.scalar.activation(dts[:, 3, :], dts[:, 2, :], ACT.Exp).then_inc(dt_act, 1)
            nc.scalar.activation(dts[:, 8, 0:16], pc("a_log", 0, 16), ACT.Exp).then_inc(dt_act, 1)
            act.wait_ge(dt_step, 4)
            nc.scalar.activation(dts[:, 5, :], dts[:, 4, :], ACT.Ln).then_inc(dt_act, 1)
            for h in range(SSM_H):
                act.wait_ge(seg_done, h + 1)
                nc.scalar.activation(seg[h % 2][:], seg[h % 2][:], ACT.Exp).then_inc(decay_done, 1)
            for g in range(2):
                act.wait_ge(y_gated, 4 * g + 4)
                nc.scalar.activation(quad[g][:], proj[:, 32 + 4 * g:36 + 4 * g, :], ACT.Square).then_inc(sq_ready, 1)
            for g in range(2):
                rms(RS["ssm"] + g)
                act.wait_ge(quad_ready, HG["ssm"] + g + 1)
                nc.scalar.activation(h_hi[:, 8 + 4 * g:12 + 4 * g, :], quad[g][:], ACT.Copy).then_inc(h_hi_done, 1)
            plain(N_OUT1, DT, acc)
            squares(acc, SQ["mix_post"], lambda g: act.wait_ge(copied, N_OUT1 + 4 * g + 4))
            rms(RS["mix_post"])
            squares(xT, SQ["ffn_pre"], lambda g: act.wait_ge(x_new, XG["mix_post"] + g + 1))
            rms(RS["ffn_pre"])
            h_upper(HG["ffn_pre"])

            with act.Fori(0, FFN_Q) as q:
                it0 = q * (FFN_STEP // 2)

                def hidden(pair, s):
                    act.wait_ge(stage_used, s + 1)
                    nc.scalar.activation(gelu_g[:], conv_g[:], ACT.Gelu_apprx_tanh).then_inc(gelu_done, 1)
                    act.wait_ge(f_raw_done, pair + 1)

                to_stage(N_FFN, it0, S_FFN, it0)
                split(N_FFN + 2, it0)
                with act.Fori(1, FQT) as i:
                    to_stage(N_FFN - 1, it0 + i, S_FFN - 1, it0 + i)
                    split(N_FFN + 1, it0 + i)
                    hidden(q * FQT + i - 1, q * FFN_STEP + i * 2 + (S_FFN - 2))
                    nc.scalar.activation(f_hi[:, bass.ds(i - 1, 1), :].rearrange("p a n -> p (a n)"), f_raw[:],
                                         ACT.Copy).then_inc(f_hi_done, 1)
                    to_stage(N_FFN, it0 + i, S_FFN, it0 + i)
                    split(N_FFN + 2, it0 + i)
                c = N_FFN + 2 * FQT
                s = S_FFN + 2 * FQT
                to_stage(c - 1, it0, s - 1, it0)
                split(c + 1, it0)
                hidden(q * FQT + FQT - 1, q * FFN_STEP + (S_FFN + 2 * FQT - 2))
                nc.scalar.activation(f_hi[:, FQT - 1, :], f_raw[:], ACT.Copy).then_inc(f_hi_done, 1)
                with act.Fori(0, DT // 2) as i:
                    for j in range(2):
                        to_stage(c + j, it0 + i, s + j, it0 + i)
                        split(c + j + 2, it0 + i)
            squares(acc, SQ["ffn_post"], lambda g: act.wait_ge(stage_used, S_FFN + FFN_Q * FFN_STEP))
            rms(RS["ffn_post"])
            squares(xT, SQ["norm1"], lambda g: act.wait_ge(x_new, XG["ffn_post"] + g + 1))
            rms(RS["norm1"])
            h_upper(HG["norm1"])
            with act.Fori(0, 15) as i:
                for j in range(2):
                    to_stage(N_IN2 + j, i, S_IN2 + j, i)
                    split(N_IN2 + j + 2, i)
            plain(N_IN2 + 30, 12, proj2, 30)

            def qk_squares(p):
                if p >= 2:
                    act.wait_ge(qk_sum, p - 1)
                nc.scalar.activation(quad[p % 2][:, 0:2, :], proj2[:, 30 + 2 * p:32 + 2 * p, :], ACT.Square
                                     ).then_inc(qk_sq, 1)

            act.wait_ge(copied, N_IN2 + IN2)
            qk_squares(0)
            for p in range(5):
                if p + 1 < 5:
                    qk_squares(p + 1)
                act.wait_ge(qk_ms, p + 1)
                if p >= 2:
                    act.wait_ge(qk_inv, p - 1)
                nc.scalar.activation(q_rms[p % 2][:], q_ms[p % 2][:], ACT.Sqrt).then_inc(qk_rms, 1)
            act.wait_ge(v2_done, 1)
            nc.scalar.activation(v2_nat[:], bank[7][:].rearrange("p (s c) -> p s c", s=TT), ACT.Copy
                                 ).then_inc(v2_copied, 1)
            for qh in range(16):
                m = qh // 2
                act.wait_ge(nmax2_done, qh + 1)
                if qh >= 2:
                    act.wait_ge(pt2_done, qh - 1)
                for tt in range(TT):
                    x = 2 * qh + tt
                    nc.scalar.activation(prob2[qh % 2][:, tt, :], bank[3 + qh % 2][:, tt * T:(tt + 1) * T], ACT.Exp,
                                         bias=soft2[:, 0, x:x + 1], scale=0.125,
                                         accum_out=soft2[:, 1, x:x + 1]).then_inc(exp2_done, 1)
                act.wait_ge(pt2_done, qh + 1)
                if qh >= 2:
                    act.wait_ge(pv2_done, qh - 1)
                nc.scalar.activation(prob2_T[qh % 2][:], bank[5 + qh % 2][:].rearrange("p (s t) -> p s t", s=TT),
                                     ACT.Copy).then_inc(pt2_copied, 1)
                if qh % 2:
                    act.wait_ge(pv2_done, qh + 1)
                    nc.scalar.activation(h_hi[:, 8 + m, :], bank[7 if m % 2 else 2][:, 0:T], ACT.Copy
                                         ).then_inc(mix2_hi, 1)

            for p in range(4):
                act.wait_ge(kk_raw, 2 * p + 2)
                if p >= 2:
                    act.wait_ge(qk_sum, HEAD_KK + p - 1)
                nc.scalar.activation(quad[p % 2][:, 0:2, :], proj2[:, 30 + 2 * p:32 + 2 * p, :], ACT.Square
                                     ).then_inc(qk_sq, 1)
            for p in range(4):
                act.wait_ge(qk_sum, HEAD_KK + p + 1)
                if p >= 2:
                    act.wait_ge(kk_done, p - 1)
                nc.scalar.activation(q_rms[p % 2][:], bank[3 + p % 2][:].rearrange("p (s t) -> p s t", s=2), ACT.Sqrt
                                     ).then_inc(qk_rms, 1)
            nc.scalar.activation(proj2[:, 28:30, :], proj2[:, 28:30, :], ACT.Sigmoid).then_inc(lora_act, 1)
            nc.scalar.activation(proj2[:, 24:26, :], proj2[:, 24:26, :], ACT.Tanh).then_inc(lora_act, 1)
            with act.Fori(0, 8) as m:
                act.wait_ge(rw_end, m + 1)
                nc.scalar.activation(v_s, tile_of(proj2, m + 16), ACT.Copy).then_inc(v_s_done, 1)
                act.wait_ge(v_s_done, m + 1)
                act.wait_ge(lora_used, m + 2)
                for w, (dst, b) in enumerate(((sig_w, bank[3]), (sig_a, bank[4]))):
                    for d in range(2):
                        nc.scalar.activation(dst[:, d, :], b[:, d * T:(d + 1) * T], ACT.Tanh, scale=0.5,
                                             bias=half_w[:, bass.ds(m + (16 * w + 8 * d), 1)]
                                             ).then_inc(tanh_done, 1)
                nc.scalar.activation(tile_of(proj2, m + 16), bank[5][:, 0:T], ACT.Copy).then_inc(g_copied, 1)
                act.wait_ge(expo_ready, m + 1)
                nc.scalar.activation(quad[0][:, 2:4, :], quad[0][:, 0:2, :], ACT.Exp, scale=-RWKV_SCALE
                                     ).then_inc(expo_done, 1)
                nc.scalar.activation(decay[:], quad[1][:, 0:2, :], ACT.Exp, scale=-RWKV_SCALE).then_inc(expo_done, 1)
                nc.scalar.activation(sig_w[:], quad[1][:, 0:2, :], ACT.Exp, scale=RWKV_SCALE).then_inc(expo_done, 1)
                act.wait_ge(n_done, m + 1)
                nc.scalar.activation(n_T, bank[4][:].rearrange("p (s t) -> p s t", t=CH), ACT.Copy
                                     ).then_inc(nT_copied, 1)
                for k in range(1, LEVELS + 1):
                    act.wait_ge(t1_done, m * LEVELS + k)
                    nc.scalar.activation(t_one, bank[5][:].rearrange("p (s t) -> p s t", t=CH), ACT.Copy
                                         ).then_inc(t1_copied, 1)
                    if k == 1:
                        for h in range(2):
                            act.wait_ge(bkn_done, m * 2 + h + 1)
                            nc.scalar.activation(bk_nat[h][:], bank[h][:].rearrange("p (s t) -> p s t", t=CH),
                                                 ACT.Copy).then_inc(bkn_copied, 1)
                for i in range(NCH):
                    act.wait_ge(w_done, m * NCH + i + 1)
                    nc.scalar.activation(w_step[:], bank[5][:, 0:P].rearrange("p (d t) -> p d t", t=CH), ACT.Copy
                                         ).then_inc(w_copied, 1)
                    act.wait_ge(u_done, m * NCH + i + 1)
                    nc.scalar.activation(uv[0][64:128, 2 * i:2 * i + 2, :],
                                         bank[6][64:128, 0:P].rearrange("p (d t) -> p d t", t=CH), ACT.Copy
                                         ).then_inc(u0_copied, 1)
                    act.wait_ge(yy_done, m * NCH + i + 1)
                    for d in range(2):
                        c = chunk_of(i, d) * CH
                        nc.scalar.activation(stage[d][:, c:c + CH], bank[1][:, d * CH:(d + 1) * CH], ACT.Copy
                                             ).then_inc(yy_copied, 1)
            for p in range(4):
                act.wait_ge(gn_centred, p + 1)
                if p >= 2:
                    act.wait_ge(qk_sum, HEAD_GN + p - 1)
                nc.scalar.activation(quad[p % 2][:, 0:2, :], proj2[:, 2 * p:2 * p + 2, :], ACT.Square
                                     ).then_inc(qk_sq, 1)
                if p:
                    act.wait_ge(qk_ms, 5 + p)
                    nc.scalar.activation(q_rms[(p - 1) % 2][:], q_ms[(p - 1) % 2][:], ACT.Sqrt).then_inc(qk_rms, 1)
                if p >= 2:
                    act.wait_ge(gn_out, p - 1)
                    nc.scalar.activation(h_hi[:, 2 * p - 4:2 * p - 2, :], quad[p % 2][:, 2:4, :], ACT.Copy
                                         ).then_inc(gn_hi, 1)
            act.wait_ge(qk_ms, 5 + 4)
            nc.scalar.activation(q_rms[1][:], q_ms[1][:], ACT.Sqrt).then_inc(qk_rms, 1)
            for p in (2, 3):
                act.wait_ge(gn_out, p + 1)
                nc.scalar.activation(h_hi[:, 2 * p:2 * p + 2, :], quad[p % 2][:, 2:4, :], ACT.Copy).then_inc(gn_hi, 1)
            plain(N_OUT2, DT, acc)
            squares(xT, SQ["norm2"], lambda g: act.wait_ge(x_new, XG["mix2"] + g + 1))
            rms(RS["norm2"])
            h_upper(HG["norm2"])
            plain(N_PQ, DT, acc)

            act.wait_ge(best_ready, 1)
            nc.scalar.activation(best_v[:], best_v[:], ACT.Exp).then_inc(gate_exp, 1)
            act.wait_ge(slots_turned, 1)
            nc.scalar.activation(slot_T[:, 0:2, :], bank[5][:].rearrange("p (x t) -> p x t", x=2), ACT.Copy
                                 ).then_inc(turned_copied, 1)
            act.wait_ge(slots_turned, 2)
            nc.scalar.activation(slot_T[:, 2, :], bank[6][:, 0:T], ACT.Copy).then_inc(turned_copied, 1)
            for b in range(T // 32):
                if b >= 2:
                    act.wait_ge(gates_stored[b % 2], 16 * (b // 2))
                by_token = g_stage[b % 2][:].rearrange("p g t e -> p t g e")
                with act.Fori(0, 4) as i:
                    for j in range(2):
                        act.wait_ge(hot_used, i * 2 + (8 * b + j + 1))
                        nc.scalar.activation(by_token[:, bass.ds(i * 8 + 4 * j, 4), :, :],
                                             bank[3 + j][:].rearrange("p (t g e) -> p t g e", t=4, e=K_TOP), ACT.Copy
                                             ).then_inc(gates_copied, 1)

            def experts(g, last=False):
                it0 = g * DT
                with act.Fori(0, DT // 2) as i:
                    for j in range(2):
                        to_stage(N_PEER + j, it0 + i, S_PEER + j, it0 + i, ACT.Gelu)
                        split(N_PEER + j + 2, it0 + i)
                        act.wait_ge(stage_used, i * 2 + (it0 * 2 + (S_PEER + j + 1)))
                        nc.scalar.activation(tile_of(p_hi, i * 2 + j), p_raw[j][:], ACT.Copy).then_inc(p_hi_done, 1)
                with act.Fori(0, DT // 2 - last) as i:
                    for j in range(2):
                        to_stage(N_PEER + DT + j, it0 + i, S_PEER + DT + j, it0 + i)
                        split(N_PEER + DT + j + 2, it0 + i)
                if last:
                    for j in range(2):
                        to_stage(N_PEER + DT + j, it0 + DT // 2 - 1, S_PEER + DT + j, it0 + DT // 2 - 1)

            with act.Fori(0, PEER_G - 1) as g:
                experts(g)
            experts(PEER_G - 1, last=True)
            squares(xT, SQ["normf"], lambda g: act.wait_ge(x_new, XG["peer"] + g + 1))
            rms(RS["normf"])

        @block.gpsimd
        def _(pool):
            nc.gpsimd.memset(relb[32:33, :], NEG).then_inc(relb_set, 1)
            for h in range(HEADS1):
                pool.wait_ge(toep_copied, h + 1)
                pool.dma_start(toep_d[h:h + 1, 0:P * 512].rearrange("a (p n) -> (a p) n", n=512), toep[h % 2][:]
                               ).then_inc(toep_out[h % 2], 16)
            for j in range(2):
                pool.wait_ge(toep_out[j], 16 * (HEADS1 // 2))
            for h in range(HEADS1):
                skew = toep_d[h:h + 1, P:P + P * 511].rearrange("a (p n) -> (a p) n", n=511)
                pool.dma_start(bias[:, h, :], skew[:, 0:T]).then_inc(bias_in, 16)
            pool.wait_ge(qk_done, 5)
            pool.dma_start(k_swap[0:64, :, :], proj2[64:128, 38:40, :]).then_inc(k_swapped, 16)
            pool.dma_start(k_swap[64:128, :, :], proj2[0:64, 38:40, :]).then_inc(k_swapped, 16)
            with pool.Fori(0, 8) as m:
                pool.wait_ge(nT_copied, m + 1)
                for k in range(1, LEVELS + 1):
                    if k >= 3:
                        pool.wait_ge(t1_done, m * LEVELS + k - 2)
                    lm = cst2[:, C2_LEVELS + 192 * k + CH:C2_LEVELS + 192 * (k + 1)]
                    nc.gpsimd.tensor_tensor(lev[k % 2].rearrange("p (i d) t -> p i (d t)", d=2),
                                            n_T.rearrange("p (i d) t -> p i (d t)", d=2),
                                            lm.unsqueeze(1).to_broadcast([P, NCH, P]), ALU.mult
                                            ).then_inc(lev_done, 1)
            pool.wait_ge(s3_done, 8)
            nc.gpsimd.memset(acc[:], 0.0).then_inc(acc_zero, 1)
            for b in range(T // 32):
                pool.wait_ge(gates_copied, 8 * (b + 1))
                pool.dma_start(gates_d[:, :, 32 * b:32 * b + 32, :].rearrange("g p t e -> p g (t e)"),
                               g_stage[b % 2][:].rearrange("p g t e -> p g (t e)")).then_inc(gates_stored[b % 2], 16)
            for j in range(2):
                pool.wait_ge(gates_stored[j], 16 * (T // 64))
            pool.dma_start(g_now[:], gates_d[0]).then_inc(g_loaded, 16)
            with pool.Fori(1, PEER_G) as g:
                pool.wait_ge(stage_used, g * PEER_STEP + (S_PEER - DT))
                pool.dma_start(g_now[:], gates_d[bass.ds(g, 1)].rearrange("a p t e -> (a p) t e")
                               ).then_inc(g_loaded, 16)

        @block.vector
        def _(dve):
            def lower(c, it):
                dve.wait_ge(hi_done, it * 2 + (c + 1))
                nc.vector.tensor_tensor(w_lo[c % 2][:], raw[c % 2][:], w_hi[c % 2][:].bitcast(F32),
                                        ALU.subtract).then_inc(lo_done, 1)

            def lowers(c, count):
                with dve.Fori(0, count // 2) as i:
                    for j in range(2):
                        lower(c + j, i)

            def rstd(i, squares_end, width):
                dve.wait_ge(sq_summed, squares_end)
                nc.vector.tensor_scalar(rb[0][:], bank[2][:, 0:T], 1.0 / width, EPS, ALU.mult, ALU.add
                                        ).then_inc(ms_done, 1)
                dve.wait_ge(rms_done, i + 1)
                nc.vector.reciprocal(rb[0][:], rb[1][:]).then_inc(rstd_done, 1)
                dve.wait_ge(rstd_done, i + 1)

            def h_lower(g, q, tile0):
                dve.wait_ge(h_hi_done, g + 1)
                nc.vector.tensor_tensor(h_lo[:, tile0:tile0 + 4, :], q, h_hi[:, tile0:tile0 + 4, :].bitcast(F32),
                                        ALU.subtract).then_inc(h_lo_done, 1)

            def normed(first, weight):
                for g in range(5):
                    if g < 4:
                        if g >= 2:
                            dve.wait_ge(h_lo_done, first + g - 1)
                        for k in range(4):
                            last = nc.vector.scalar_tensor_tensor(
                                quad[g % 2][:, k, :], xT[:, 4 * g + k, :], pc(weight, 4 * g + k), rb[0][:],
                                ALU.mult, ALU.mult)
                        last.then_inc(quad_ready, 1)
                    if g:
                        h_lower(first + g - 1, quad[(g - 1) % 2][:], 4 * g - 4)

            def renew(weight, scaled0):
                for g in range(4):
                    for k in range(4):
                        last = nc.vector.scalar_tensor_tensor(acc[:, 4 * g + k, :], acc[:, 4 * g + k, :],
                                                              pc(weight, 4 * g + k), rb[0][:], ALU.mult, ALU.mult)
                    last.then_inc(acc_done, 1)
                for g in range(4):
                    dve.wait_ge(acc_done, scaled0 + g + 1)
                    nc.vector.tensor_tensor(xT[:, 4 * g:4 * g + 4, :], xT[:, 4 * g:4 * g + 4, :],
                                            acc[:, 4 * g:4 * g + 4, :], ALU.add).then_inc(x_new, 1)

            dve.wait_ge(s_par, 16)
            dve.wait_ge(s_x, 64)
            rstd(RS["mix_pre"], SQ["mix_pre"] + 4, D)
            normed(HG["mix_pre"], "ln_mix_pre")
            lower(0, 0)
            lower(1, 0)
            lowers(2, 32)
            with dve.Fori(0, 6) as i:
                for j in range(2):
                    dst = proj[:, bass.ds(i * 2 + (32 + j), 1), :].rearrange("p a n -> p (a n)")
                    tile = i * 2 + j

                    def col(tap):
                        return par[:, bass.ds(i * 2 + (PCOL["ssm_conv_w"] + 12 * tap + j), 1)]
                    dve.wait_ge(copied, i * 2 + (33 + j))
                    nc.vector.tensor_scalar(dst, stage[j][:], col(3),
                                            par[:, bass.ds(i * 2 + (PCOL["ssm_conv_b"] + j), 1)],
                                            ALU.mult, ALU.add).then_inc(conv_step, 1)
                    for tap in (2, 1, 0):
                        lag = 3 - tap
                        dve.wait_ge(conv_step, tile * 3 + lag)
                        o = proj[:, bass.ds(i * 2 + (32 + j), 1), lag:T].rearrange("p a n -> p (a n)")
                        nc.vector.scalar_tensor_tensor(o, stage[j][:, 0:T - lag], col(tap), o, ALU.mult, ALU.add
                                                       ).then_inc(conv_step if lag < 3 else stage_used, 1)
                    lower(34 + j, i)
            lower(46, 0)

            def logits(u):
                h, i = u // 2, u % 2
                w = (i + 1) * P
                dve.wait_ge(score_done, u + 1)
                if u >= 2:
                    dve.wait_ge(exp_done, u - 1)
                nc.vector.scalar_tensor_tensor(logit[i][:, 0:w], bank[3 + i][:, 0:w], float(P) ** -0.5,
                                               bias[:, h, T - w:T] if i else bias[:, h, P:T],
                                               ALU.mult, ALU.add).then_inc(logit_done, 1)
                dve.wait_ge(logit_done, u + 1)
                nc.vector.tensor_reduce(soft[:, 3, u:u + 1], logit[i][:, 0:w], AX, ALU.max).then_inc(max_done, 1)
                dve.wait_ge(max_done, u + 1)
                nc.vector.tensor_scalar(soft[:, 0, u:u + 1], soft[:, 3, u:u + 1], -1.0, None, ALU.mult
                                        ).then_inc(nmax_done, 1)

            dve.wait_ge(bias_in, 16 * HEADS1)
            logits(0)
            for u in range(2 * HEADS1):
                h, i = u // 2, u % 2
                w = (i + 1) * P
                if u + 1 < 2 * HEADS1:
                    logits(u + 1)
                dve.wait_ge(exp_done, u + 1)
                nc.vector.reciprocal(soft[:, 2, u:u + 1], soft[:, 1, u:u + 1]).then_inc(rsum_done, 1)
                dve.wait_ge(rsum_done, u + 1)
                nc.vector.tensor_scalar(prob[i][:, 0:w], prob[i][:, 0:w], soft[:, 2, u:u + 1], None, ALU.mult
                                        ).then_inc(prob_done, 1)
                if i:
                    dve.wait_ge(mix_hi, h + 1)
                    nc.vector.tensor_tensor(h_lo[:, h, :], bank[7][:, 0:T], h_hi[:, h, :].bitcast(F32),
                                            ALU.subtract).then_inc(mix_lo, 1)

            step = [0]

            def dt_op(ins):
                ins.then_inc(dt_step, 1)
                step[0] += 1
                dve.wait_ge(dt_step, step[0])

            dve.wait_ge(dt_tr, 1)
            dt_op(nc.vector.tensor_tensor(dts[:, 0, :].rearrange("p (s h) -> p s h", s=TT),
                                          bank[3][:, 0:32].rearrange("p (s h) -> p s h", s=TT),
                                          pc("dt_bias", 0, 16).unsqueeze(1).to_broadcast([P, TT, SSM_H]), ALU.add))
            dt_op(nc.vector.tensor_scalar(dts[:, 1, :], dts[:, 0, :], -1.0, None, ALU.mult))
            dt_op(nc.vector.tensor_tensor(dts[:, 2, :], dts[:, 0, :], dts[:, 1, :], ALU.min))
            dve.wait_ge(dt_act, 1)
            dt_op(nc.vector.tensor_scalar(dts[:, 4, :], dts[:, 3, :], 1.0, None, ALU.add))
            dt_op(nc.vector.tensor_scalar(dts[:, 1, :], dts[:, 4, :], -1.0, None, ALU.add))
            dt_op(nc.vector.tensor_tensor(dts[:, 1, :], dts[:, 3, :], dts[:, 1, :], ALU.subtract))
            dt_op(nc.vector.reciprocal(dts[:, 6, :], dts[:, 4, :]))
            dt_op(nc.vector.tensor_tensor(dts[:, 1, :], dts[:, 1, :], dts[:, 6, :], ALU.mult))
            dve.wait_ge(dt_act, 3)
            dt_op(nc.vector.tensor_tensor(dts[:, 1, :], dts[:, 1, :], dts[:, 5, :], ALU.add))
            dt_op(nc.vector.scalar_tensor_tensor(dts[:, 6, :], dts[:, 0, :], 0.0, dts[:, 1, :], ALU.max, ALU.add))
            dt_op(nc.vector.tensor_scalar(dts[:, 8, 16:32], dts[:, 8, 0:16], -1.0, None, ALU.mult))
            dt_op(nc.vector.tensor_tensor(dts[:, 7, :].rearrange("p (s h) -> p s h", s=TT),
                                          dts[:, 6, :].rearrange("p (s h) -> p s h", s=TT),
                                          dts[:, 8, 16:32].unsqueeze(1).to_broadcast([P, TT, SSM_H]), ALU.mult))
            dve.wait_ge(acs_done, 1)
            acs = dts[:, 2, :]
            dt_op(nc.vector.tensor_copy(acs, bank[4][:, 0:32]))
            for u in range(4):
                st, half = u // 2, u % 2
                dve.wait_ge(xn_done, u + 1)
                nc.vector.tensor_tensor(x_dt[:, st, 8 * half:8 * half + 8, :],
                                        bank[5 + u % 2][:].rearrange("p (h d) -> p h d", d=64),
                                        dts[:, 6, st * 16 + 8 * half:st * 16 + 8 * half + 8].unsqueeze(2)
                                        .to_broadcast([P, 8, 64]), ALU.mult).then_inc(xdt_done, 1)
            for g in range(2):
                dve.wait_ge(cb_done, g + 1)
                nc.vector.tensor_tensor(cb[:, g, 0:T], bank[7][:, 0:T], causal, ALU.mult).then_inc(cb_masked, 1)
                nc.vector.tensor_tensor(cb[:, g, T:T + P], bank[7][:, T:T + P], causal[:, 0:P],
                                        ALU.mult).then_inc(cb_masked, 1)

            def segments(h):
                dve.wait_ge(acsb_done, h + 1)
                if h >= 2:
                    dve.wait_ge(mt_done, h - 1)
                b = bank[3 + h % 2]
                nc.vector.tensor_scalar(seg[h % 2][:, 0:T], b[:, 0:T], acs[:, h:h + 1], 0.0,
                                        ALU.subtract, ALU.min)
                nc.vector.tensor_scalar(seg[h % 2][:, T:T + P], b[:, P:T], acs[:, 16 + h:17 + h], 0.0,
                                        ALU.subtract, ALU.min).then_inc(seg_done, 1)

            dve.wait_ge(cb_masked, 4)
            dve.wait_ge(silu_done, 5)
            segments(0)
            for h in range(SSM_H):
                if h + 1 < SSM_H:
                    segments(h + 1)
                dve.wait_ge(decay_done, h + 1)
                if h >= 2:
                    dve.wait_ge(y_done, h - 1)
                nc.vector.tensor_tensor(mt[h % 2][:], seg[h % 2][:], cb[:, h // 8, :], ALU.mult
                                        ).then_inc(mt_done, 1)
                if h % 2 == 0 and h:
                    m = h // 2 - 1
                    dve.wait_ge(y_done, 2 * m + 2)
                    nc.vector.scalar_tensor_tensor(proj[:, 32 + m, :], proj[:, 32 + m, :], pc("d_skip", m),
                                                   bank[5 + m % 2][:, 0:T], ALU.mult, ALU.add).then_inc(y_read, 1)
                    dve.wait_ge(y_read, m + 1)
                    nc.vector.tensor_tensor(proj[:, 32 + m, :], proj[:, 32 + m, :], proj[:, 24 + m, :], ALU.mult
                                            ).then_inc(y_gated, 1)
            m = 7
            dve.wait_ge(y_done, 2 * m + 2)
            nc.vector.scalar_tensor_tensor(proj[:, 32 + m, :], proj[:, 32 + m, :], pc("d_skip", m),
                                           bank[5 + m % 2][:, 0:T], ALU.mult, ALU.add).then_inc(y_read, 1)
            dve.wait_ge(y_read, m + 1)
            nc.vector.tensor_tensor(proj[:, 32 + m, :], proj[:, 32 + m, :], proj[:, 24 + m, :], ALU.mult
                                    ).then_inc(y_gated, 1)
            dve.wait_ge(y_gated, 8)
            for g in range(2):
                rstd(RS["ssm"] + g, SQ["ssm"] + g + 1, D // 4)
                dve.wait_ge(sq_summed, SQ["ssm"] + g + 1)
                for k in range(4):
                    last = nc.vector.scalar_tensor_tensor(quad[g][:, k, :], proj[:, 32 + 4 * g + k, :],
                                                          pc("ssm_norm_w", 4 * g + k), rb[0][:], ALU.mult, ALU.mult)
                last.then_inc(quad_ready, 1)
                h_lower(HG["ssm"] + g, quad[g][:], 8 + 4 * g)
            lowers(N_OUT1 + 2, DT)
            rstd(RS["mix_post"], SQ["mix_post"] + 4, D)
            renew("ln_mix_post", 0)
            rstd(RS["ffn_pre"], SQ["ffn_pre"] + 4, D)
            normed(HG["ffn_pre"], "ln_ffn_pre")

            nc.vector.memset(acc[:], 0.0).then_inc(acc_done, 1)
            dve.wait_ge(acc_done, 5)
            with dve.Fori(0, FFN_Q) as q:
                it0 = q * (FFN_STEP // 2)

                def conv(i):
                    pair = q * FQT + i
                    dve.wait_ge(copied, it0 * 2 + i * 2 + (N_FFN + 2))
                    outs = (conv_g, conv_u)
                    for tap in (2, 1, 0):
                        lag = 2 - tap
                        for s in range(2):
                            w = par[:, bass.ds(q * FQT + i + (PCOL["ffn_conv_w"] + 88 * tap + 44 * s), 1)]
                            if lag == 0:
                                b = par[:, bass.ds(q * FQT + i + (PCOL["ffn_conv_b"] + 44 * s), 1)]
                                ins = nc.vector.tensor_scalar(outs[s][:], stage[s][:], w, b, ALU.mult, ALU.add)
                                ins.then_inc(pair_step, 1)
                            else:
                                dve.wait_ge(pair_step, pair * 4 + (s + 1 + 2 * (lag - 1)))
                                ins = nc.vector.scalar_tensor_tensor(
                                    outs[s][:, lag:T], stage[s][:, 0:T - lag], w, outs[s][:, lag:T],
                                    ALU.mult, ALU.add)
                                ins.then_inc(pair_step if lag == 1 else stage_used, 1)

                def product(i, dst_lo, dst_hi):
                    pair = q * FQT + i
                    dve.wait_ge(gelu_done, pair + 1)
                    dve.wait_ge(stage_used, q * FFN_STEP + i * 2 + (S_FFN + 2))
                    nc.vector.tensor_tensor(f_raw[:], gelu_g[:], conv_u[:], ALU.mult).then_inc(f_raw_done, 1)
                    dve.wait_ge(f_hi_done, pair + 1)
                    nc.vector.tensor_tensor(dst_lo, f_raw[:], dst_hi.bitcast(F32), ALU.subtract
                                            ).then_inc(f_lo_done, 1)

                lower(N_FFN + 2, it0)
                with dve.Fori(1, FQT) as i:
                    conv(i - 1)
                    lower(N_FFN + 1, it0 + i)
                    product(i - 1, f_lo[:, bass.ds(i - 1, 1), :].rearrange("p a n -> p (a n)"),
                            f_hi[:, bass.ds(i - 1, 1), :].rearrange("p a n -> p (a n)"))
                    lower(N_FFN + 2, it0 + i)
                c = N_FFN + 2 * FQT
                conv(FQT - 1)
                lower(c + 1, it0)
                product(FQT - 1, f_lo[:, FQT - 1, :], f_hi[:, FQT - 1, :])
                with dve.Fori(0, DT // 2) as i:
                    for j in range(2):
                        dve.wait_ge(copied, (it0 + i) * 2 + (c + j + 1))
                        d = acc[:, bass.ds(i * 2 + j, 1), :].rearrange("p a n -> p (a n)")
                        nc.vector.tensor_tensor(d, d, stage[j][:], ALU.add).then_inc(stage_used, 1)
                        lower(c + j + 2, it0 + i)
            dve.wait_ge(stage_used, S_FFN + FFN_Q * FFN_STEP)
            rstd(RS["ffn_post"], SQ["ffn_post"] + 4, D)
            renew("ln_ffn_post", 5)
            rstd(RS["norm1"], SQ["norm1"] + 4, D)
            normed(HG["norm1"], "norm1")

            prep = Chain(dve, prep2, 0)
            dve.wait_ge(s_par, 16)
            n = prep.step(nc.vector.tensor_tensor(shift_c, pc("mu_prev", 0, 30), pc("mu_next", 0, 30), ALU.add))
            prep.wait(n)
            prep.step(nc.vector.tensor_scalar(shift_c, shift_c, -1.0, 1.0, ALU.mult, ALU.add))
            prep.step(nc.vector.tensor_scalar(half_w, pc("w0", 0, 32), 0.5, None, ALU.mult))
            prep.step(nc.vector.tensor_scalar(omka, pc("k_a", 0, 8), -1.0, 1.0, ALU.mult, ALU.add))
            n = prep.step(nc.vector.tensor_scalar(half_rk, pc("r_k", 0, 8), 0.5, None, ALU.mult))
            prep.wait(n)
            with dve.Fori(0, 15) as i:
                for j in range(2):
                    dst = proj2[:, bass.ds(i * 2 + j, 1), :]
                    z = stage[j]
                    dve.wait_ge(copied, i * 2 + (N_IN2 + j + 1))
                    nc.vector.tensor_scalar(dst.rearrange("p a n -> p (a n)"), z[:],
                                            small2[:, bass.ds(i * 2 + j, 1)], None, ALU.mult
                                            ).then_inc(shift_step, 1)
                    dve.wait_ge(shift_step, i * 4 + (2 * j + 1))
                    o = proj2[:, bass.ds(i * 2 + j, 1), 1:T].rearrange("p a n -> p (a n)")
                    nc.vector.scalar_tensor_tensor(o, z[:, 0:T - 1],
                                                   par[:, bass.ds(i * 2 + (PCOL["mu_prev"] + j), 1)], o,
                                                   ALU.mult, ALU.add).then_inc(shift_step, 1)
                    dve.wait_ge(shift_step, i * 4 + (2 * j + 2))
                    o = proj2[:, bass.ds(i * 2 + j, 1), 0:T - 1].rearrange("p a n -> p (a n)")
                    nc.vector.scalar_tensor_tensor(o, z[:, 1:T],
                                                   par[:, bass.ds(i * 2 + (PCOL["mu_next"] + j), 1)], o,
                                                   ALU.mult, ALU.add).then_inc(stage_used, 1)
                    lower(N_IN2 + j + 2, i)
            lowers(N_IN2 + 32, 12)

            dve.wait_ge(cst2_loaded, 16)
            cos2 = cst2[:, C2_COS:C2_COS + T].unsqueeze(1).to_broadcast([P, 2, T])
            sin2 = cst2[:, C2_SIN:C2_SIN + T].unsqueeze(1).to_broadcast([P, 2, T])

            def qk_mean(p):
                if p >= 2:
                    dve.wait_ge(qk_done, p - 1)
                dve.wait_ge(qk_sum, p + 1)
                nc.vector.tensor_scalar(q_ms[p % 2][:], bank[3 + p % 2][:].rearrange("p (s t) -> p s t", s=2),
                                        1.0 / 64, EPS, ALU.mult, ALU.add).then_inc(qk_ms, 1)

            qk_mean(0)
            for p in range(5):
                if p + 1 < 5:
                    qk_mean(p + 1)
                x = proj2[:, 30 + 2 * p:32 + 2 * p, :]
                ms = q_ms[p % 2]
                dve.wait_ge(qk_rms, p + 1)
                nc.vector.reciprocal(ms[:], q_rms[p % 2][:]).then_inc(qk_inv, 1)
                dve.wait_ge(qk_inv, p + 1)
                nc.vector.scalar_tensor_tensor(x, x, pc("q_norm") if p < 4 else pc("k_norm"), ms[:],
                                               ALU.mult, ALU.mult).then_inc(qk_norm, 1)
                dve.wait_ge(qk_turned, p + 1)
                nc.vector.tensor_tensor(ms[:], bank[5 + p % 2][:].rearrange("p (s t) -> p s t", s=2), sin2, ALU.mult
                                        ).then_inc(qk_step, 1)
                nc.vector.tensor_tensor(x, x, cos2, ALU.mult).then_inc(qk_step, 1)
                dve.wait_ge(qk_step, 2 * p + 2)
                nc.vector.tensor_tensor(x, x, ms[:], ALU.add).then_inc(qk_done, 1)

            def maxima(qh):
                x = 2 * qh
                dve.wait_ge(s2_done, qh + 1)
                nc.vector.tensor_reduce(soft2[:, 3, x:x + 2], bank[3 + qh % 2][:].rearrange("p (s t) -> p s t", s=TT),
                                        AX, ALU.max).then_inc(max2_done, 1)
                dve.wait_ge(max2_done, qh + 1)
                nc.vector.tensor_scalar(soft2[:, 0, x:x + 2], soft2[:, 3, x:x + 2], -0.125, None, ALU.mult
                                        ).then_inc(nmax2_done, 1)

            maxima(0)
            for qh in range(16):
                m, x = qh // 2, 2 * qh
                if qh + 1 < 16:
                    maxima(qh + 1)
                dve.wait_ge(exp2_done, x + 2)
                nc.vector.reciprocal(soft2[:, 2, x:x + 2], soft2[:, 1, x:x + 2]).then_inc(rsum2_done, 1)
                dve.wait_ge(rsum2_done, qh + 1)
                for tt in range(TT):
                    last = nc.vector.tensor_scalar(prob2[qh % 2][:, tt, :], prob2[qh % 2][:, tt, :],
                                                   soft2[:, 2, x + tt:x + tt + 1], None, ALU.mult)
                last.then_inc(prob2_done, 1)
                if qh % 2:
                    dve.wait_ge(mix2_hi, m + 1)
                    nc.vector.tensor_tensor(h_lo[:, 8 + m, :], bank[7 if m % 2 else 2][:, 0:T],
                                            h_hi[:, 8 + m, :].bitcast(F32), ALU.subtract).then_inc(mix2_lo, 1)

            for t in range(8):
                nc.vector.tensor_scalar(proj2[:, 30 + t, :], proj2[:, 8 + t, :], pc("k_k", t), None, ALU.mult
                                        ).then_inc(kk_raw, 1)
            for p in range(4):
                x, ms = proj2[:, 30 + 2 * p:32 + 2 * p, :], q_ms[p % 2]
                dve.wait_ge(qk_rms, HEAD_KK + p + 1)
                nc.vector.tensor_scalar(ms[:], q_rms[p % 2][:], 1e-12, None, ALU.max).then_inc(kk_step, 1)
                dve.wait_ge(kk_step, 2 * p + 1)
                nc.vector.reciprocal(ms[:], ms[:]).then_inc(kk_step, 1)
                dve.wait_ge(kk_step, 2 * p + 2)
                nc.vector.tensor_tensor(x, x, ms[:], ALU.mult).then_inc(kk_done, 1)
            dve.wait_ge(kk_done, 4)
            nc.vector.memset(state[0][:], 0.0).then_inc(lora_used, 1)
            nc.vector.memset(state[1][:], 0.0).then_inc(rw_end, 1)
            RW_STEPS = 17
            with dve.Fori(0, 8) as m:
                rw = Chain(dve, rw_dve, RW_STEPS, m)
                dve.wait_ge(rw_end, m + 1)
                dve.wait_ge(tanh_done, m * 4 + 4)
                n = rw.step(nc.vector.tensor_scalar(sig_w[:], sig_w[:], 0.5, 0.5, ALU.mult, ALU.add))
                rw.step(nc.vector.tensor_scalar(sig_a[:], sig_a[:], 0.5, 0.5, ALU.mult, ALU.add))
                rw.wait(n)
                upto, before = quad[1][:, 0:2, :], quad[0][:, 0:2, :]
                rw.step(nc.vector.tensor_tensor_scan(quad[1][:, 0, :], reset, sig_w[:, 0, :], 0.0, ALU.mult, ALU.add))
                n = rw.step(nc.vector.tensor_tensor_scan(quad[1][:, 1, :], reset, sig_w[:, 1, :], 0.0,
                                                         ALU.mult, ALU.add))
                rw.wait(n)
                back = quad[1][:, 1, :].rearrange("p (c t) -> p c t", t=CH)
                rw.step(nc.vector.tensor_tensor(quad[0][:, 0, :], quad[1][:, 0, :], sig_w[:, 0, :], ALU.subtract))
                n = rw.step(nc.vector.tensor_tensor(quad[0][:, 1, :].rearrange("p (c t) -> p c t", t=CH),
                                                    back[:, :, CH - 1:CH].to_broadcast([P, NCH, CH]), back,
                                                    ALU.subtract))
                rw.wait(n)
                nc.vector.tensor_tensor(quad[1][:, 1, :], quad[0][:, 1, :], sig_w[:, 1, :], ALU.add
                                        ).then_inc(expo_ready, 1)
                kd, ka = bk[:, 1, :, :], bk[:, 0, :, :]
                kb, kkb = twice(proj2, m + 8), twice(proj2, m + 30)
                n = rw.step(nc.vector.tensor_scalar(kd, sig_a[:], par[:, bass.ds(m + PCOL["k_a"], 1)],
                                                    small2[:, bass.ds(m + 62, 1)], ALU.mult, ALU.add))
                rw.step(nc.vector.tensor_tensor(ka, sig_a[:], kkb, ALU.mult))
                rw.wait(n)
                n = rw.step(nc.vector.tensor_tensor(kd, kd, kb, ALU.mult))
                rw.wait(n)
                n = rw.step(nc.vector.tensor_tensor(quad[1][:, 3, :], bk[:, 1, 0, :], bk[:, 1, 1, :], ALU.add))
                rw.wait(n)
                nc.vector.scalar_tensor_tensor(quad[1][:, 3, :], quad[1][:, 3, :], small2[:, bass.ds(m + 70, 1)],
                                               tile_of(proj2, m), ALU.mult, ALU.mult).then_inc(rk_done, 1)
                dve.wait_ge(expo_done, m * 3 + 3)
                rw.step(nc.vector.scalar_tensor_tensor(ar[:, 0, :, :], quad[0][:, 2:4, :], -1.0, kkb,
                                                       ALU.mult, ALU.mult))
                rw.step(nc.vector.tensor_tensor(ar[:, 1, :, :], decay[:], twice(proj2, m), ALU.mult))
                rw.step(nc.vector.tensor_tensor(kd, kd, sig_w[:], ALU.mult))
                nc.vector.tensor_tensor(ka, ka, sig_w[:], ALU.mult).then_inc(scaled_done, 1)
                dve.wait_ge(vn_done, m + 1)
                for h in range(2):
                    r = 64 * h
                    nc.vector.tensor_copy(uv[h][r:r + 64, :, :],
                                          bank[6][r:r + 64, :].rearrange("p (s t) -> p s t", t=CH)
                                          ).then_inc(uv_v, 1)
                dve.wait_ge(bonus_sum, m + 1)
                rw.step(nc.vector.tensor_tensor(tile_of(proj2, m + 8), bank[7][:, 0:T], v_s, ALU.mult))
                dve.wait_ge(n_done, m + 1)
                for dst, b, off in ((inv, bank[3], 0), (inv_T, bank[4], CH)):
                    if off:
                        dve.wait_ge(nT_copied, m + 1)
                    lm = cst2[:, C2_LEVELS + off:C2_LEVELS + off + P].unsqueeze(1).to_broadcast([P, NCH, P])
                    n = rw.step(nc.vector.tensor_tensor(dst[:].rearrange("p (i d) t -> p i (d t)", d=2),
                                                        b[:].rearrange("p (i x) -> p i x", x=P), lm, ALU.mult))
                rw.wait(n)
                eyes = eye.unsqueeze(1).to_broadcast([P, 8, CH])
                rw.step(nc.vector.tensor_tensor(inv[:], inv[:], eyes, ALU.add))
                nc.vector.tensor_tensor(inv_T[:], inv_T[:], eyes, ALU.add).then_inc(x_new2, 1)

                def mask_pairs(u, h, half, b):
                    dve.wait_ge(pairs_done, m * 4 + u)
                    mask = cst2[:, C2_PAIRS:C2_PAIRS + 2 * P].unsqueeze(1).to_broadcast([P, 2, 2 * P])
                    nc.vector.tensor_tensor(
                        pairs[h][:, 4 * half:4 * half + 4, :].rearrange("p (i d) t -> p i (d t)", d=2),
                        b[:].rearrange("p (i x) -> p i x", x=2 * P), mask, ALU.mult).then_inc(pairs_masked, 1)

                for k in range(1, LEVELS + 1):
                    dve.wait_ge(x_done, m * LEVELS + k)
                    dve.wait_ge(x_new2, m * (LEVELS + 1) + k)
                    if k < LEVELS:
                        nc.vector.tensor_tensor(inv[:], inv[:], bank[6][:].rearrange("p (s t) -> p s t", t=CH), ALU.add)
                    nc.vector.tensor_tensor(inv_T[:], inv_T[:], bank[7][:].rearrange("p (s t) -> p s t", t=CH),
                                            ALU.add).then_inc(x_new2, 1)
                    if k >= 2:
                        mask_pairs(k - 1, (k - 2) % 2, (k - 2) // 2, bank[(0, 0, 2, 3, 4, 0)[k]])
                nc.vector.memset(state[0][:], 0.0).then_inc(state_new, 1)
                for i in range(NCH):
                    old, new = state[i % 2], state[(i + 1) % 2]
                    if i < NCH - 1:
                        dve.wait_ge(state_new, m * NCH + i + 1)
                        for d in range(2):
                            at = chunk_of(i, d) * CH + (CH - 1 if d == 0 else 0)
                            last = nc.vector.tensor_scalar(state_w[:, d, :], old[:, d, :], decay[:, d, at:at + 1],
                                                           None, ALU.mult)
                        last.then_inc(st_scaled, 1)
                    dve.wait_ge(u_done, m * NCH + i + 1)
                    nc.vector.tensor_copy(uv[1][0:64, 2 * i:2 * i + 2, :],
                                          bank[6][0:64, 0:P].rearrange("p (d t) -> p d t", t=CH)
                                          ).then_inc(u1_copied, 1)
                    if i < NCH - 1:
                        dve.wait_ge(st_scaled, m * (NCH - 1) + i + 1)
                        dve.wait_ge(s_done, m * (NCH - 1) + i + 1)
                        for d in range(2):
                            at = chunk_of(i, d) * CH + (CH - 1 if d == 0 else 0)
                            last = nc.vector.scalar_tensor_tensor(
                                new[:, d, :], bank[7][:, d * CH:(d + 1) * CH], decay[:, d, at:at + 1],
                                state_w[:, d, :], ALU.mult, ALU.add)
                        last.then_inc(state_new, 1)
                dve.wait_ge(yy_copied, m * (2 * NCH) + 2 * NCH)
                nc.vector.tensor_tensor(tile_of(proj2, m), stage[0][:], stage[1][:], ALU.add).then_inc(rw_end, 1)
                assert rw.n == RW_STEPS, rw.n

            gn = Chain(dve, gn_step, 0)

            def centre(p):
                dve.wait_ge(gn_mean, p + 1)
                x = proj2[:, 2 * p:2 * p + 2, :]
                nc.vector.scalar_tensor_tensor(x, bank[3 + p % 2][:].rearrange("p (s t) -> p s t", s=2), -1.0 / 64, x,
                                               ALU.mult, ALU.add).then_inc(gn_centred, 1)

            def variance(p):
                dve.wait_ge(qk_sum, HEAD_GN + p + 1)
                nc.vector.tensor_scalar(q_ms[p % 2][:], bank[5 + p % 2][:].rearrange("p (s t) -> p s t", s=2),
                                        1.0 / 64, GN_EPS, ALU.mult, ALU.add).then_inc(qk_ms, 1)

            def gn_lower(p):
                dve.wait_ge(gn_hi, p + 1)
                nc.vector.tensor_tensor(h_lo[:, 2 * p:2 * p + 2, :], quad[p % 2][:, 2:4, :],
                                        h_hi[:, 2 * p:2 * p + 2, :].bitcast(F32), ALU.subtract).then_inc(mix2_lo, 1)

            dve.wait_ge(rw_end, 9)
            centre(0)
            variance(0)
            for p in range(4):
                if p + 1 < 4:
                    centre(p + 1)
                    variance(p + 1)
                x, ms = proj2[:, 2 * p:2 * p + 2, :], q_ms[p % 2]
                dve.wait_ge(qk_rms, HEAD_GN + p + 1)
                gn.wait(gn.step(nc.vector.reciprocal(ms[:], q_rms[p % 2][:])))
                gn.wait(gn.step(nc.vector.tensor_tensor(x, x, ms[:], ALU.mult)))
                for t in (2 * p, 2 * p + 1):
                    n = gn.step(nc.vector.tensor_scalar(proj2[:, t, :], proj2[:, t, :], pc("lnx_w", t), pc("lnx_b", t),
                                                        ALU.mult, ALU.add))
                gn.wait(n)
                gn.wait(gn.step(nc.vector.tensor_tensor(x, x, proj2[:, 8 + 2 * p:10 + 2 * p, :], ALU.add)))
                if p >= 2:
                    gn_lower(p - 2)
                    dve.wait_ge(mix2_lo, 8 + p - 1)
                nc.vector.tensor_tensor(quad[p % 2][:, 2:4, :], x, proj2[:, 16 + 2 * p:18 + 2 * p, :], ALU.mult
                                        ).then_inc(gn_out, 1)
            gn_lower(2)
            gn_lower(3)
            lowers(N_OUT2 + 2, DT)
            dve.wait_ge(copied, N_OUT2 + DT)
            for g in range(4):
                nc.vector.tensor_tensor(xT[:, 4 * g:4 * g + 4, :], xT[:, 4 * g:4 * g + 4, :],
                                        acc[:, 4 * g:4 * g + 4, :], ALU.add).then_inc(x_new, 1)
            rstd(RS["norm2"], SQ["norm2"] + 4, D)
            normed(HG["norm2"], "norm2")
            lowers(N_PQ + 2, DT)

            top = Chain(dve, top_step, 0)
            for u in range(8):
                tt, grp = u // 4, u % 4
                dve.wait_ge(s3_done, u + 1)
                parts = [(bank[3 + u % 2][:, x * P:(x + 1) * P], rest[:, x, 0:P],
                          top_v[:, tt, 4 * grp + x, :], top_i[:, tt, 4 * grp + x, :]) for x in range(4)]
                for s, r, v, n in parts:
                    k = top.step(nc.vector.max(v[:, 0:8], s))
                top.wait(k)
                for s, r, v, n in parts:
                    top.step(nc.vector.max_index(n[:, 0:8], v[:, 0:8], s))
                for s, r, v, n in parts:
                    last = nc.vector.match_replace(r, v[:, 0:8], s, LOWEST)
                last.then_inc(bank_read, 1)
                dve.wait_ge(bank_read, u + 1)
                for s, r, v, n in parts:
                    k = top.step(nc.vector.max(v[:, 8:16], r))
                top.wait(k)
                for s, r, v, n in parts:
                    k = top.step(nc.vector.max_index(n[:, 8:16], v[:, 8:16], r))
            top.wait(k)
            top.step(nc.vector.tensor_copy(top_f[:], top_i[:]))
            for tt in range(TT):
                v = top_v[:, tt].rearrange("p (h s) k -> p h s k", s=2)
                k = top.step(nc.vector.tensor_tensor(
                    cand[:].rearrange("p h (i j) -> p h i j", j=K_TOP),
                    v[:, :, 0, :].unsqueeze(3).to_broadcast([P, PEER_H, K_TOP, K_TOP]),
                    v[:, :, 1, :].unsqueeze(2).to_broadcast([P, PEER_H, K_TOP, K_TOP]), ALU.add))
                top.wait(k)
                for h in range(PEER_H):
                    k = top.step(nc.vector.max(best_v[:, tt, h, 0:8], cand[:, h, :]))
                top.wait(k)
                for h in range(PEER_H):
                    top.step(nc.vector.max_index(best_i[:, tt, h, 0:8], best_v[:, tt, h, 0:8], cand[:, h, :]))
                for h in range(PEER_H):
                    k = top.step(nc.vector.match_replace(rest[:, h, :], best_v[:, tt, h, 0:8], cand[:, h, :], LOWEST))
                top.wait(k)
                for h in range(PEER_H):
                    k = top.step(nc.vector.max(best_v[:, tt, h, 8:16], rest[:, h, :]))
                top.wait(k)
                for h in range(PEER_H):
                    k = top.step(nc.vector.max_index(best_i[:, tt, h, 8:16], best_v[:, tt, h, 8:16], rest[:, h, :]))
            top.wait(k)
            bests = best_v[:].rearrange("p s h k -> p (s h) k")
            lead = gate_s[:, 0, :].unsqueeze(2)
            k = top.step(nc.vector.tensor_copy(lead, bests[:, :, 0:1]))
            top.wait(k)
            nc.vector.tensor_tensor(bests, bests, lead.to_broadcast([P, TT * PEER_H, K_TOP]), ALU.subtract
                                    ).then_inc(best_ready, 1)
            numbers = best_i[:].rearrange("p s h k -> p s (h k)")
            top.step(nc.vector.tensor_scalar(half_i[:, 0], numbers, 4, None, ALU.logical_shift_right))
            k = top.step(nc.vector.tensor_scalar(half_i[:, 1], numbers, 15, None, ALU.bitwise_and))
            top.wait(k)
            k = top.step(nc.vector.tensor_copy(half_f[:], half_i[:]))
            top.wait(k)
            for side in range(2):
                for tt in range(TT):
                    k = top.step(nc.vector.tensor_tensor(
                        hot[:], half_f[:, side, tt, :].unsqueeze(2).to_broadcast([P, SLOTS, K_TOP]),
                        count[:, P:P + K_TOP].unsqueeze(1).to_broadcast([P, SLOTS, K_TOP]), ALU.is_equal))
                    top.wait(k)
                    of = top_f[:, tt].rearrange("p (h s) k -> p h s k", s=2)[:, :, side, :]
                    hots = hot[:].rearrange("p (h k) i -> p h k i", h=PEER_H)
                    k = top.step(nc.vector.tensor_tensor(
                        hots, hots, of.unsqueeze(2).to_broadcast([P, PEER_H, K_TOP, K_TOP]), ALU.mult))
                    top.wait(k)
                    k = top.step(nc.vector.tensor_reduce(slot[:, side, tt, :], hot[:], AX, ALU.add))
                    top.wait(k)
            dve.wait_ge(gate_exp, 1)
            k = top.step(nc.vector.tensor_reduce(gate_s[:, 0, :], bests, AX, ALU.add))
            top.wait(k)
            k = top.step(nc.vector.reciprocal(gate_s[:, 1, :], gate_s[:, 0, :]))
            top.wait(k)
            nc.vector.tensor_tensor(slot[:, 2].rearrange("p s (h k) -> p (s h) k", k=K_TOP), bests,
                                    gate_s[:, 1, :].unsqueeze(2).to_broadcast([P, TT * PEER_H, K_TOP]), ALU.mult
                                    ).then_inc(slots_done, 1)
            dve.wait_ge(turned_copied, 2)
            dve.wait_ge(count_loaded, 16)
            def one_hots(i, j, first=False):
                if not first:
                    dve.wait_ge(hot_used, i * 2 + (j - 1))
                nc.vector.tensor_tensor(
                    hot_col[j][:], count[:, 0:P].unsqueeze(1).to_broadcast([P, 4, P]),
                    slot_T[:, 1, bass.ds(i * 8 + 4 * j, 4)].unsqueeze(2).to_broadcast([P, 4, P]), ALU.is_equal)
                for x in range(4):
                    def col(which):
                        return slot_T[:, which, bass.ds(i * 8 + (4 * j + x), 1)]
                    last = nc.vector.tensor_scalar(hot_row[j][:, x, :], count[:, 0:P], col(0), col(2),
                                                   ALU.is_equal, ALU.mult)
                last.then_inc(hot_ready, 1)

            for j in range(2):
                one_hots(0, j, first=True)
            with dve.Fori(1, T // 8) as i:
                for j in range(2):
                    one_hots(i, j)

            def experts(g, last=False):
                it0 = g * DT
                with dve.Fori(0, DT // 2) as i:
                    dve.wait_ge(g_loaded, g * 16 + 16)
                    for j in range(2):
                        dve.wait_ge(copied, it0 * 2 + i * 2 + (N_PEER + j + 1))
                        nc.vector.tensor_tensor(p_raw[j][:], stage[j][:],
                                                g_now[:, :, bass.ds(i * 2 + j, 1)].rearrange("p t e -> p (t e)"),
                                                ALU.mult).then_inc(stage_used, 1)
                        lower(N_PEER + j + 2, it0 + i)
                        dve.wait_ge(p_hi_done, it0 + i * 2 + (j + 1))
                        nc.vector.tensor_tensor(tile_of(p_lo, i * 2 + j), p_raw[j][:],
                                                tile_of(p_hi, i * 2 + j).bitcast(F32), ALU.subtract
                                                ).then_inc(p_lo_done, 1)

                def add(i, j):
                    dve.wait_ge(copied, (it0 + i) * 2 + (N_PEER + DT + j + 1))
                    d = tile_of(acc, i * 2 + j)
                    nc.vector.tensor_tensor(d, d, stage[j][:], ALU.add).then_inc(stage_used, 1)

                with dve.Fori(0, DT // 2 - last) as i:
                    for j in range(2):
                        add(i, j)
                        lower(N_PEER + DT + j + 2, it0 + i)
                if last:
                    for j in range(2):
                        add(DT // 2 - 1, j)

            dve.wait_ge(acc_zero, 1)
            with dve.Fori(0, PEER_G - 1) as g:
                experts(g)
            experts(PEER_G - 1, last=True)
            dve.wait_ge(stage_used, S_PEER + PEER_G * PEER_STEP)
            for g in range(4):
                nc.vector.tensor_tensor(xT[:, 4 * g:4 * g + 4, :], xT[:, 4 * g:4 * g + 4, :],
                                        acc[:, 4 * g:4 * g + 4, :], ALU.add).then_inc(x_new, 1)
            rstd(RS["normf"], SQ["normf"] + 4, D)
            for g in range(4):
                if g >= 2:
                    dve.wait_ge(out_stored[g % 2], 16)
                for k in range(4):
                    last = nc.vector.scalar_tensor_tensor(quad[g % 2][:, k, :], xT[:, 4 * g + k, :],
                                                          pc("normf", 4 * g + k), rb[0][:], ALU.mult, ALU.mult)
                last.then_inc(out_ready, 1)


def panels(w, ntiles, ktiles):
    return np.ascontiguousarray(
        w.reshape(ktiles, P, ntiles, P).transpose(2, 1, 0, 3)).reshape(ntiles, P, ktiles * P)


def by_channel(v):
    return np.asarray(v).reshape(-1, P).T


def tokens_last(x):
    return np.ascontiguousarray(x.T.reshape(-1, P, x.shape[0]).transpose(1, 0, 2))


def pad_columns(w, widths):
    pieces, at = [], 0
    for n in widths:
        pieces.append(w[..., at:at + n])
        if n % P:
            pieces.append(np.zeros((*w.shape[:-1], P - n % P), w.dtype))
        at += n
    return np.concatenate(pieces, axis=-1)


RWKV_PARTS = (1024, 1024, 1024, 96, 96, 96, 96, 256)


def lay_out(i):
    i = {k: np.asarray(v) for k, v in i.items()}
    arrays = {"consts1": consts1(), "x": tokens_last(i["x"][0]), "rel_bias": i["rel_bias"]}
    arrays["w_in1"] = panels(pad_columns(i["w_in"][0], (5632, 16)), 45, DT)
    arrays["w_out1"] = panels(i["w_out"][0], DT, DT)
    up = i["w_ffn_up"][0].reshape(D, 2, 44, P).transpose(0, 2, 1, 3).reshape(D, 88 * P)
    arrays["w_up"] = panels(up, 88, DT)
    arrays["w_down"] = np.concatenate([panels(w, DT, FQT) for w in np.split(i["w_ffn_down"][0], FFN_Q)])
    arrays["w_out2"] = panels(i["w_out_2"][0], DT, DT)
    arrays["consts2"] = consts2()
    arrays["consts3"] = consts3()
    arrays["w_pq"] = panels(i["w_pq_2"][0], DT, DT)
    arrays["sub_keys"] = np.ascontiguousarray(i["sub_keys_2"][0].transpose(3, 0, 1, 2)).reshape(P, 2 * PEER_H, P)
    arrays["u_tab"] = np.ascontiguousarray(
        i["u_tab_2"][0].reshape(P, P, DT, P).transpose(0, 3, 2, 1)).reshape(P, P, PW)
    arrays["v_tab"] = np.ascontiguousarray(
        i["v_tab_2"][0].reshape(PEER_G, DT, P, DT, P).transpose(0, 3, 2, 1, 4)).reshape(P, P, PW)
    low = np.zeros((8, P, 6, P), i["w2_2"].dtype)
    for n, name in enumerate(("w2_2", "a2_2")):
        for d in range(2):
            low[:, 0:96, 2 * n + d, :] = i[name][0, d].reshape(96, 8, P).transpose(1, 0, 2)
    for k in range(2):
        low[:, :, 4 + k, :] = i["g2_2"][0, k * P:(k + 1) * P].reshape(P, 8, P).transpose(1, 0, 2)
    arrays["lora"] = low
    arrays["w_in2"] = panels(pad_columns(i["w_in_2"][0], (*RWKV_PARTS, 1536)), IN2, DT)
    cols = [
        by_channel(i["ln_mix_pre"]), by_channel(i["ln_mix_post"]), by_channel(i["ln_ffn_pre"]),
        by_channel(i["ln_ffn_post"]), by_channel(i["ssm_conv_w"]), by_channel(i["ssm_conv_b"]),
        by_channel(i["ssm_norm_w"]), by_channel(np.repeat(i["d_skip"], 64)),
        by_channel(i["ffn_conv_w"]), by_channel(i["ffn_conv_b"]),
        np.broadcast_to(i["dt_bias"], (P, 16)), np.broadcast_to(i["a_log"], (P, 16)),
        by_channel(pad_columns(i["mu_prev_2"][0], RWKV_PARTS)), by_channel(pad_columns(i["mu_next_2"][0], RWKV_PARTS)),
        by_channel(i["w0_2"]), by_channel(i["a0_2"]), by_channel(i["k_k_2"]), by_channel(i["k_a_2"]),
        by_channel(i["r_k_2"]), by_channel(i["lnx_w_2"]), by_channel(i["lnx_b_2"]),
        np.tile(i["q_norm_w_2"][0], 2)[:, None], np.tile(i["k_norm_w_2"][0], 2)[:, None],
        by_channel(i["norm1_w_2"]), by_channel(i["norm2_w_2"]), by_channel(i["normf_w_2"]),
    ]
    arrays["params"] = np.ascontiguousarray(np.concatenate(cols, axis=1))
    return arrays


def kernel(**inputs):
    import concourse.bacc as _bacc
    from concourse.bass_utils import run_bass_kernel_spmd as _run

    nc = _bacc.Bacc("TRN2", target_bir_lowering=False, num_devices=1)
    arrays = lay_out(inputs)
    a = {k: nc.dram_tensor(f"in_{k}", v.shape, mybir.dt.from_np(v.dtype), kind="ExternalInput").ap()
         for k, v in arrays.items()}
    out = nc.dram_tensor("out", (P, DT, T), F32, kind="ExternalOutput").ap()
    build(nc, a, out)
    r = _run(nc, [{f"in_{k}": v for k, v in arrays.items()}], core_ids=[0])
    return r.results[0]["out"].transpose(2, 1, 0).reshape(1, T, D)
```
